# Optimizing a Trainium2 kernel written in Bass

```python
import math
import jax
import jax.numpy as jnp
from jax import lax
import numpy as np
import jax, jax.numpy as jnp

D_MODEL = 1024
BATCH = 1
SEQ = 256
DEPTH = 2

GRID_W = 64
CTX_LEN = 256
HEAD_DIM = 64
Q_BLOCK = 128
EPS = 1e-6
ROPE_THETA = 10000.0
D_FF = 2816
ADA_STD = 0.02
N_MOD = 9

A_HEADS = 8
A_KV_HEADS = 2
B_HEADS = 8
B_NOPE = 64
B_ROPE = 32
B_VDIM = 64
B_KV_RANK = 256
B_QK = B_NOPE + B_ROPE
C_HEADS = 8
C_DK = 64
C_DV = 64
C_CHUNK = 64
D_HEADS = 8
D_WIN_H = 8
D_WIN_W = 16

N_EVEN = (DEPTH + 1) // 2
N_ODD = DEPTH // 2

A_QW = A_HEADS * HEAD_DIM
A_KVW = A_KV_HEADS * HEAD_DIM
B_QW = B_HEADS * B_QK
AB_IN = A_QW + 2 * A_KVW + B_QW + B_KV_RANK + B_ROPE
AB_SPLITS = (A_QW, A_QW + A_KVW, A_QW + 2 * A_KVW, A_QW + 2 * A_KVW + B_QW, A_QW + 2 * A_KVW + B_QW + B_KV_RANK)
AB_OUT = A_QW + B_HEADS * B_VDIM

C_W = C_HEADS * C_DK
C_VW = C_HEADS * C_DV
D_W = D_HEADS * HEAD_DIM
CD_IN = 3 * C_W + 2 * C_VW + 3 * D_W
CD_SPLITS = (C_W, 2 * C_W, 3 * C_W, 3 * C_W + C_VW, 3 * C_W + 2 * C_VW, 3 * C_W + 2 * C_VW + D_W, 3 * C_W + 2 * C_VW + 2 * D_W)
CD_OUT = C_VW + D_W


def rms_norm(x, g):
    xf = x.astype(jnp.float32)
    y = xf * lax.rsqrt(jnp.mean(xf * xf, axis=-1, keepdims=True) + EPS)
    return (y * g.astype(jnp.float32)).astype(x.dtype)

def modulate(h, shift, scale):
    return h * (1 + scale[:, None, :]) + shift[:, None, :]

def swiglu(h, w1, w3, w2):
    return (jax.nn.silu(h @ w1) * (h @ w3)) @ w2

def half_ffn(h, g, shift, scale, gate, w1, w3, w2):
    return h + 0.5 * gate[:, None, :] * swiglu(modulate(rms_norm(h, g), shift, scale), w1, w3, w2)

def rope_1d(pos, dim):
    inv = ROPE_THETA ** (-jnp.arange(0, dim, 2, dtype=jnp.float32) / dim)
    ang = pos.astype(jnp.float32)[:, None] * inv[None, :]
    ang = jnp.concatenate([ang, ang], axis=-1)
    return jnp.cos(ang), jnp.sin(ang)

def axial_rope_tables(n_tok, dim):
    t = jnp.arange(n_tok, dtype=jnp.int32)
    cos_r, sin_r = rope_1d(t // GRID_W, dim // 2)
    cos_c, sin_c = rope_1d(t % GRID_W, dim // 2)
    return jnp.concatenate([cos_r, cos_c], axis=-1), jnp.concatenate([sin_r, sin_c], axis=-1)

def _rotate_half(u):
    u1, u2 = jnp.split(u, 2, axis=-1)
    return jnp.concatenate([-u2, u1], axis=-1)

def apply_axial_rope(x, cos, sin):
    h = x.shape[-1] // 2
    rot = jnp.concatenate([_rotate_half(x[..., :h]), _rotate_half(x[..., h:])], axis=-1)
    return x * cos[None, :, None, :].astype(x.dtype) + rot * sin[None, :, None, :].astype(x.dtype)

def blocked_attention(q, k, v, scale):
    b, s, hkv, g, d = q.shape
    nb = s // Q_BLOCK
    qb = jnp.moveaxis(q.reshape(b, nb, Q_BLOCK, hkv, g, d), 1, 0)

    def one_block(qi):
        sc = jnp.einsum('bqhgd,bkhd->bhgqk', qi, k, preferred_element_type=jnp.float32) * scale
        p = jax.nn.softmax(sc, axis=-1).astype(v.dtype)
        return jnp.einsum('bhgqk,bkhd->bqhgd', p, v)

    out = lax.map(one_block, qb)
    return jnp.moveaxis(out, 0, 1).reshape(b, s, hkv * g * v.shape[-1])

def mixer_ab(hx, hc, w_in, a_qn, a_kn, b_qn, b_kn, b_kvn, b_wukv, w_out, with_ctx):
    b, s, _ = hx.shape
    grp = A_HEADS // A_KV_HEADS
    cos_a, sin_a = axial_rope_tables(s, HEAD_DIM)
    cos_b, sin_b = axial_rope_tables(s, B_ROPE)

    def project(h, rotary):
        n = h.shape[1]
        aq, ak, av, bq, bkv, bkr = jnp.split(h @ w_in, AB_SPLITS, axis=-1)
        aq = rms_norm(aq.reshape(b, n, A_HEADS, HEAD_DIM), a_qn)
        ak = rms_norm(ak.reshape(b, n, A_KV_HEADS, HEAD_DIM), a_kn)
        av = av.reshape(b, n, A_KV_HEADS, HEAD_DIM)
        kv = (rms_norm(bkv, b_kvn) @ b_wukv).reshape(b, n, B_HEADS, B_NOPE + B_VDIM)
        bk_rope = jnp.broadcast_to(bkr[:, :, None, :], (b, n, B_HEADS, B_ROPE))
        bq = rms_norm(bq.reshape(b, n, B_HEADS, B_QK), b_qn)
        bk = rms_norm(jnp.concatenate([kv[..., :B_NOPE], bk_rope], axis=-1), b_kn)
        bv = kv[..., B_NOPE:]
        if rotary:
            aq = apply_axial_rope(aq, cos_a, sin_a)
            ak = apply_axial_rope(ak, cos_a, sin_a)
            bq = jnp.concatenate([bq[..., :B_NOPE], apply_axial_rope(bq[..., B_NOPE:], cos_b, sin_b)], axis=-1)
            bk = jnp.concatenate([bk[..., :B_NOPE], apply_axial_rope(bk[..., B_NOPE:], cos_b, sin_b)], axis=-1)
        return aq.reshape(b, n, A_KV_HEADS, grp, HEAD_DIM), ak, av, bq[:, :, :, None, :], bk, bv

    qa, ka, va, qb, kb, vb = project(hx, True)
    qa_c, ka_c, va_c, qb_c, kb_c, vb_c = project(hc, False)
    y_x = jnp.concatenate([
        blocked_attention(qa, jnp.concatenate([ka, ka_c], axis=1), jnp.concatenate([va, va_c], axis=1), HEAD_DIM ** -0.5),
        blocked_attention(qb, jnp.concatenate([kb, kb_c], axis=1), jnp.concatenate([vb, vb_c], axis=1), B_QK ** -0.5),
    ], axis=-1) @ w_out
    if not with_ctx:
        return y_x, None
    y_c = jnp.concatenate([
        blocked_attention(qa_c, ka_c, va_c, HEAD_DIM ** -0.5),
        blocked_attention(qb_c, kb_c, vb_c, B_QK ** -0.5),
    ], axis=-1) @ w_out
    return y_x, y_c

def hgrn_chunk_scan(q, k, v, g, s0, with_output):
    b, h, n, dk = q.shape
    nc = n // C_CHUNK

    def chunks(t):
        return jnp.moveaxis(t.reshape(b, h, nc, C_CHUNK, t.shape[-1]), 2, 0)

    tri = jnp.tril(jnp.ones((C_CHUNK, C_CHUNK), dtype=bool))[:, :, None]

    def step(state, inp):
        qi, ki, vi, gi = inp
        gcum = jnp.cumsum(gi, axis=2)
        glast = gcum[:, :, -1, :]
        new_state = jnp.exp(glast)[..., None] * state + jnp.einsum('bhck,bhcv->bhkv', ki * jnp.exp(glast[:, :, None, :] - gcum), vi)
        if not with_output:
            return new_state, None
        o_inter = jnp.einsum('bhtk,bhkv->bhtv', qi * jnp.exp(gcum), state)
        decay = jnp.exp(jnp.where(tri, gcum[:, :, :, None, :] - gcum[:, :, None, :, :], -jnp.inf))
        attn = jnp.einsum('bhtk,bhsk,bhtsk->bhts', qi, ki, decay)
        return new_state, o_inter + jnp.einsum('bhts,bhsv->bhtv', attn, vi)

    s_fin, o = lax.scan(step, s0, (chunks(q), chunks(k), chunks(v), chunks(g)))
    if with_output:
        o = jnp.moveaxis(o, 0, 2).reshape(b, h, n, v.shape[-1])
    return s_fin, o

def neighbourhood_attention(q, k, v, k_ctx, v_ctx, rpb):
    b, s, h, d = q.shape
    rows = s // GRID_W
    kh = min(D_WIN_H, rows)
    kw = D_WIN_W
    n_win = kh * kw
    cols = np.arange(GRID_W)
    col_idx = np.clip(cols - kw // 2, 0, GRID_W - kw)[:, None] + np.arange(kw)[None, :]
    col_rel = col_idx - cols[:, None] + (D_WIN_W - 1)
    rpb_cols = rpb[:, :, col_rel]
    kg = k.reshape(b, rows, GRID_W, h, d)
    vg = v.reshape(b, rows, GRID_W, h, d)
    q_rows = jnp.moveaxis(q.reshape(b, rows, GRID_W, h, d), 1, 0)
    scale = d ** -0.5

    def one_row(args):
        r, q_row = args
        rs = jnp.clip(r - kh // 2, 0, rows - kh)
        k_win = lax.dynamic_slice_in_dim(kg, rs, kh, axis=1)[:, :, col_idx]
        v_win = lax.dynamic_slice_in_dim(vg, rs, kh, axis=1)[:, :, col_idx]
        row_rel = rs + jnp.arange(kh) - r + (D_WIN_H - 1)
        bias = jnp.transpose(jnp.take(rpb_cols, row_rel, axis=1), (0, 2, 1, 3))
        s_win = jnp.einsum('bchd,brcwhd->bhcrw', q_row, k_win, preferred_element_type=jnp.float32) * scale + bias[None].astype(jnp.float32)
        s_ctx = jnp.einsum('bchd,bnhd->bhcn', q_row, k_ctx, preferred_element_type=jnp.float32) * scale
        p = jax.nn.softmax(jnp.concatenate([s_win.reshape(b, h, GRID_W, n_win), s_ctx], axis=-1), axis=-1).astype(v.dtype)
        return (jnp.einsum('bhcrw,brcwhd->bchd', p[..., :n_win].reshape(b, h, GRID_W, kh, kw), v_win)
                + jnp.einsum('bhcn,bnhd->bchd', p[..., n_win:], v_ctx))

    out = lax.map(one_row, (jnp.arange(rows, dtype=jnp.int32), q_rows))
    return jnp.moveaxis(out, 0, 1).reshape(b, s, h * d)

def mixer_cd(hx, hc, w_in, lb, c_gn, d_qn, d_kn, d_rpb, w_out, with_ctx):
    b, s, _ = hx.shape
    f32 = jnp.float32
    px = jnp.split(hx @ w_in, CD_SPLITS, axis=-1)
    pc = jnp.split(hc @ w_in, CD_SPLITS, axis=-1)

    def heads_first(t, dh):
        return jnp.moveaxis(t.reshape(b, t.shape[1], -1, dh), 2, 1)

    def hgrn_inputs(p, direction):
        z = p[1 + direction].astype(f32)
        lbd = lb[direction]
        logf = jnp.logaddexp(jnp.log(lbd), jnp.log1p(-lbd) + jax.nn.log_sigmoid(z))
        key_in = -jnp.expm1(logf)
        t = (heads_first(jax.nn.silu(p[0].astype(f32)), C_DK), heads_first(key_in, C_DK),
             heads_first(p[3].astype(f32), C_DV), heads_first(logf, C_DK))
        if direction == 1:
            t = tuple(jnp.flip(u, axis=2) for u in t)
        return t

    def hgrn_out(o, p):
        o = jnp.moveaxis(o, 1, 2)
        n = o.shape[1]
        gate = p[4].reshape(b, n, C_HEADS, C_DV)
        return (rms_norm(o, c_gn).astype(gate.dtype) * jax.nn.silu(gate)).reshape(b, n, C_VW)

    s0 = jnp.zeros((b, C_HEADS, C_DK, C_DV), f32)
    qf, kf, vf, gf = hgrn_inputs(pc, 0)
    s_cf, o_cf = hgrn_chunk_scan(qf, kf, vf, gf, s0, with_ctx)
    qf, kf, vf, gf = hgrn_inputs(px, 0)
    _, o_xf = hgrn_chunk_scan(qf, kf, vf, gf, s_cf, True)
    qb_, kb_, vb_, gb_ = hgrn_inputs(pc, 1)
    s_cb, o_cb = hgrn_chunk_scan(qb_, kb_, vb_, gb_, s0, with_ctx)
    qb_, kb_, vb_, gb_ = hgrn_inputs(px, 1)
    _, o_xb = hgrn_chunk_scan(qb_, kb_, vb_, gb_, s_cb, True)
    o_lat = o_xf + jnp.flip(o_xb, axis=2)

    def d_qkv(p):
        n = p[5].shape[1]
        return (rms_norm(p[5].reshape(b, n, D_HEADS, HEAD_DIM), d_qn),
                rms_norm(p[6].reshape(b, n, D_HEADS, HEAD_DIM), d_kn),
                p[7].reshape(b, n, D_HEADS, HEAD_DIM))

    dq, dk, dv = d_qkv(px)
    dq_c, dk_c, dv_c = d_qkv(pc)
    y_x = jnp.concatenate([hgrn_out(o_lat, px), neighbourhood_attention(dq, dk, dv, dk_c, dv_c, d_rpb)], axis=-1) @ w_out
    if not with_ctx:
        return y_x, None
    o_ctx = o_cf + jnp.flip(o_cb, axis=2)
    y_c = jnp.concatenate([hgrn_out(o_ctx, pc), blocked_attention(dq_c[:, :, :, None, :], dk_c, dv_c, HEAD_DIM ** -0.5)], axis=-1) @ w_out
    return y_x, y_c

def first_inputs(seed: int = 0) -> dict:
    key = jax.random.key(seed)
    ks = jax.random.split(key, 26)

    def nrm(k, shape, scale):
        return jax.random.normal(k, shape, jnp.float32) * scale

    def gain(k, shape):
        return 1.0 + 0.05 * jax.random.normal(k, shape, jnp.float32)

    return {
        'x': nrm(ks[0], (BATCH, SEQ, D_MODEL), 1.0),
        'c': nrm(ks[1], (BATCH, D_MODEL), 1.0),
        'ctx': nrm(ks[2], (BATCH, CTX_LEN, D_MODEL), 1.0),
        'c_ctx': nrm(ks[3], (D_MODEL,), 1.0),
        'norm_g': gain(ks[4], (DEPTH, 3, D_MODEL)),
        'ada_w': nrm(ks[5], (DEPTH, D_MODEL, N_MOD * D_MODEL), ADA_STD),
        'ada_b': nrm(ks[6], (DEPTH, N_MOD * D_MODEL), 0.02),
        'ffn_w1': nrm(ks[7], (DEPTH, 2, D_MODEL, D_FF), D_MODEL ** -0.5),
        'ffn_w3': nrm(ks[8], (DEPTH, 2, D_MODEL, D_FF), D_MODEL ** -0.5),
        'ffn_w2': nrm(ks[9], (DEPTH, 2, D_FF, D_MODEL), D_FF ** -0.5),
        'ab_w_in': nrm(ks[10], (N_EVEN, D_MODEL, AB_IN), D_MODEL ** -0.5),
        'ab_a_qn': gain(ks[11], (N_EVEN, HEAD_DIM)),
        'ab_a_kn': gain(ks[12], (N_EVEN, HEAD_DIM)),
        'ab_b_qn': gain(ks[13], (N_EVEN, B_QK)),
        'ab_b_kn': gain(ks[14], (N_EVEN, B_QK)),
        'ab_b_kvn': gain(ks[15], (N_EVEN, B_KV_RANK)),
        'ab_b_wukv': nrm(ks[16], (N_EVEN, B_KV_RANK, B_HEADS * (B_NOPE + B_VDIM)), B_KV_RANK ** -0.5),
        'ab_w_out': nrm(ks[17], (N_EVEN, AB_OUT, D_MODEL), AB_OUT ** -0.5),
        'cd_w_in': nrm(ks[18], (N_ODD, D_MODEL, CD_IN), D_MODEL ** -0.5),
        'hgrn_lb': nrm(ks[19], (DEPTH, 2, C_W), 0.5),
        'cd_c_gn': gain(ks[20], (N_ODD, C_DV)),
        'cd_d_qn': gain(ks[21], (N_ODD, HEAD_DIM)),
        'cd_d_kn': gain(ks[22], (N_ODD, HEAD_DIM)),
        'cd_d_rpb': nrm(ks[23], (N_ODD, D_HEADS, 2 * D_WIN_H - 1, 2 * D_WIN_W - 1), 0.5),
        'cd_w_out': nrm(ks[24], (N_ODD, CD_OUT, D_MODEL), CD_OUT ** -0.5),
    }

def first_block(x, c, ctx, c_ctx, norm_g, ada_w, ada_b, ffn_w1, ffn_w3, ffn_w2, ab_w_in, ab_a_qn, ab_a_kn, ab_b_qn, ab_b_kn, ab_b_kvn, ab_b_wukv, ab_w_out, cd_w_in, hgrn_lb, cd_c_gn, cd_d_qn, cd_d_kn, cd_d_rpb, cd_w_out):
    lb_all = jnp.cumsum(jax.nn.softmax(hgrn_lb.astype(jnp.float32), axis=0), axis=0)
    lb_all = lb_all - lb_all[:1]
    for l in range(DEPTH):
        last = l == DEPTH - 1
        i = l // 2
        mod_x = jnp.split(jax.nn.silu(c) @ ada_w[l] + ada_b[l], N_MOD, axis=-1)
        mod_c = jnp.split(jax.nn.silu(c_ctx)[None, :] @ ada_w[l] + ada_b[l], N_MOD, axis=-1)
        x = half_ffn(x, norm_g[l, 0], mod_x[0], mod_x[1], mod_x[2], ffn_w1[l, 0], ffn_w3[l, 0], ffn_w2[l, 0])
        ctx = half_ffn(ctx, norm_g[l, 0], mod_c[0], mod_c[1], mod_c[2], ffn_w1[l, 0], ffn_w3[l, 0], ffn_w2[l, 0])
        hx = modulate(rms_norm(x, norm_g[l, 1]), mod_x[3], mod_x[4])
        hc = modulate(rms_norm(ctx, norm_g[l, 1]), mod_c[3], mod_c[4])
        if l % 2 == 0:
            y_x, y_c = mixer_ab(hx, hc, ab_w_in[i], ab_a_qn[i], ab_a_kn[i], ab_b_qn[i], ab_b_kn[i], ab_b_kvn[i], ab_b_wukv[i], ab_w_out[i], not last)
        else:
            y_x, y_c = mixer_cd(hx, hc, cd_w_in[i], lb_all[l], cd_c_gn[i], cd_d_qn[i], cd_d_kn[i], cd_d_rpb[i], cd_w_out[i], not last)
        x = x + mod_x[5][:, None, :] * y_x
        x = half_ffn(x, norm_g[l, 2], mod_x[6], mod_x[7], mod_x[8], ffn_w1[l, 1], ffn_w3[l, 1], ffn_w2[l, 1])
        if not last:
            ctx = ctx + mod_c[5][:, None, :] * y_c
            ctx = half_ffn(ctx, norm_g[l, 2], mod_c[6], mod_c[7], mod_c[8], ffn_w1[l, 1], ffn_w3[l, 1], ffn_w2[l, 1])
    return x


NEG = -1e30
D_FF_2 = 4 * D_MODEL
N_MEM = 256
MEM_HEADS = 4
NSA_HEADS = 12
NSA_KV_HEADS = 3
NSA_GQA = NSA_HEADS // NSA_KV_HEADS
CMP_BLOCK = 32
CMP_STRIDE = 16
CMP_HIDDEN = 256
SEL_BLOCK = 64
SEL_TOPK = 16
WINDOW = 512
NSA_Q_BLOCK = 32
SEL_FORCE = 1e9
DIL_PATTERNS = ((128, 1), (512, 4), (2048, 16))
N_DIL_GROUPS = 3
DIL_SLOTS = 8
DIL_Q_BLOCK = 64
N_A_LAYERS = DEPTH // 2
N_B_LAYERS = DEPTH - N_A_LAYERS
MEM_W = MEM_HEADS * HEAD_DIM
A_Q = NSA_HEADS * HEAD_DIM
A_KV = NSA_KV_HEADS * HEAD_DIM
A_GATES = 3 * NSA_HEADS
A_IN = A_Q + 6 * A_KV + MEM_W + A_GATES
A_OUT = A_Q + MEM_W
A_SPLITS = (A_Q, A_Q + A_KV, A_Q + 2 * A_KV, A_Q + 3 * A_KV, A_Q + 4 * A_KV, A_Q + 5 * A_KV, A_Q + 6 * A_KV, A_Q + 6 * A_KV + MEM_W)
B_Q = N_DIL_GROUPS * DIL_SLOTS * HEAD_DIM
B_IN = B_Q + MEM_W
B_OUT = DIL_SLOTS * HEAD_DIM + MEM_W
SHARED_KV = 2 * DIL_SLOTS * HEAD_DIM


def rmsnorm(x, g):
    x32 = x.astype(jnp.float32)
    y = x32 * lax.rsqrt(jnp.mean(x32 * x32, axis=-1, keepdims=True) + EPS)
    return (y * g.astype(jnp.float32)).astype(x.dtype)

def rope(x, pos):
    half = x.shape[-1] // 2
    inv_freq = ROPE_THETA ** (-jnp.arange(half, dtype=jnp.float32) / half)
    ang = jnp.asarray(pos, jnp.float32)[:, None] * inv_freq[None, :]
    cos = jnp.cos(ang).astype(x.dtype)
    sin = jnp.sin(ang).astype(x.dtype)
    x1, x2 = x[..., :half], x[..., half:]
    return jnp.concatenate([x1 * cos - x2 * sin, x1 * sin + x2 * cos], axis=-1)

def split_heads(x, n):
    b, s, _ = x.shape
    return x.reshape(b, s, n, HEAD_DIM).transpose(0, 2, 1, 3)

def merge_heads(x):
    b, h, s, d = x.shape
    return x.transpose(0, 2, 1, 3).reshape(b, s, h * d)

def chunk_seq(x, axis, size):
    shp = x.shape
    x = x.reshape(shp[:axis] + (shp[axis] // size, size) + shp[axis + 1:])
    return jnp.moveaxis(x, axis, 0)

def unchunk_seq(y, axis):
    y = jnp.moveaxis(y, 0, axis)
    shp = y.shape
    return y.reshape(shp[:axis] + (shp[axis] * shp[axis + 1],) + shp[axis + 2:])

def masked_softmax(s, mask):
    return jax.nn.softmax(jnp.where(mask, s.astype(jnp.float32), NEG), axis=-1)

def nsa_attention(q, k_cmp, v_cmp, k_sel, v_sel, k_win, v_win, gate_logits,
                  q_norm, k_norm, cmp_pos, cmp_w1, cmp_b1, cmp_w2, cmp_b2):
    B, S, _ = q.shape
    G, R, D, QB = NSA_KV_HEADS, NSA_GQA, HEAD_DIM, NSA_Q_BLOCK
    scale = D ** -0.5
    pos = jnp.arange(S)
    q = rope(rmsnorm(split_heads(q, NSA_HEADS), q_norm), pos).reshape(B, G, R, S, D)
    k_sel = rope(rmsnorm(split_heads(k_sel, G), k_norm[1]), pos)
    v_sel = split_heads(v_sel, G)
    k_win = rope(rmsnorm(split_heads(k_win, G), k_norm[2]), pos)
    v_win = split_heads(v_win, G)

    n_cmp = (S - CMP_BLOCK) // CMP_STRIDE + 1
    blk_tok = np.arange(n_cmp)[:, None] * CMP_STRIDE + np.arange(CMP_BLOCK)[None, :]
    cmp_end = jnp.asarray(blk_tok[:, -1], jnp.int32)

    def compress(t, i):
        tb = (t[:, :, blk_tok] + cmp_pos[i]).reshape(B, G, n_cmp, CMP_BLOCK * D)
        return jax.nn.gelu(tb @ cmp_w1[i] + cmp_b1[i]) @ cmp_w2[i] + cmp_b2[i]

    k_c = rope(rmsnorm(compress(split_heads(k_cmp, G), 0), k_norm[0]), cmp_end)
    v_c = compress(split_heads(v_cmp, G), 1)

    n_blk = S // SEL_BLOCK
    n_sel = min(SEL_TOPK, n_blk)
    c_start = np.arange(n_cmp)[:, None] * CMP_STRIDE
    b_start = np.arange(n_blk)[None, :] * SEL_BLOCK
    overlap = jnp.asarray((c_start < b_start + SEL_BLOCK) & (c_start + CMP_BLOCK > b_start), jnp.float32)
    k_sel_blk = k_sel.reshape(B, G, n_blk, SEL_BLOCK, D)
    v_sel_blk = v_sel.reshape(B, G, n_blk, SEL_BLOCK, D)
    k_win_pad = jnp.pad(k_win, ((0, 0), (0, 0), (WINDOW, 0), (0, 0)))
    v_win_pad = jnp.pad(v_win, ((0, 0), (0, 0), (WINDOW, 0), (0, 0)))
    b_ix = jnp.arange(B)[:, None, None, None]
    g_ix = jnp.arange(G)[None, :, None, None]
    blk_ids = jnp.arange(n_blk)

    gates = jax.nn.sigmoid(gate_logits).reshape(B, S, NSA_HEADS, 3)
    gates = gates.transpose(0, 2, 1, 3).reshape(B, G, R, S, 3)

    def block(args):
        c, q_b, g_b = args
        t = c * QB + jnp.arange(QB)
        m_c = cmp_end[None, :] <= t[:, None]
        p_c = masked_softmax(jnp.einsum('bgrqd,bgcd->bgrqc', q_b, k_c) * scale, m_c)
        o_c = jnp.einsum('bgrqc,bgcd->bgrqd', p_c.astype(v_c.dtype), v_c)
        o_c = jnp.where(m_c.any(-1)[:, None], o_c, 0)
        imp = jnp.einsum('bgqc,cj->bgqj', p_c.sum(axis=2), overlap)
        cur = (t // SEL_BLOCK)[:, None]
        forced = (blk_ids == 0) | (blk_ids == cur) | (blk_ids == cur - 1)
        imp = jnp.where(forced, SEL_FORCE, jnp.where(blk_ids <= cur, imp, NEG))
        top_v, top_i = lax.top_k(imp, n_sel)
        k_g = k_sel_blk[b_ix, g_ix, top_i].reshape(B, G, QB, n_sel * SEL_BLOCK, D)
        v_g = v_sel_blk[b_ix, g_ix, top_i].reshape(B, G, QB, n_sel * SEL_BLOCK, D)
        key_pos = top_i[..., None] * SEL_BLOCK + jnp.arange(SEL_BLOCK)
        m_s = (key_pos <= t[:, None, None]) & (top_v > NEG / 2)[..., None]
        m_s = m_s.reshape(B, G, 1, QB, n_sel * SEL_BLOCK)
        p_s = masked_softmax(jnp.einsum('bgrqd,bgqkd->bgrqk', q_b, k_g) * scale, m_s)
        o_s = jnp.einsum('bgrqk,bgqkd->bgrqd', p_s.astype(v_g.dtype), v_g)
        k_b = lax.dynamic_slice_in_dim(k_win_pad, c * QB, QB + WINDOW, axis=2)
        v_b = lax.dynamic_slice_in_dim(v_win_pad, c * QB, QB + WINDOW, axis=2)
        kpos = c * QB - WINDOW + jnp.arange(QB + WINDOW)
        dist = t[:, None] - kpos[None, :]
        m_w = (kpos[None, :] >= 0) & (dist >= 0) & (dist < WINDOW)
        p_w = masked_softmax(jnp.einsum('bgrqd,bgkd->bgrqk', q_b, k_b) * scale, m_w)
        o_w = jnp.einsum('bgrqk,bgkd->bgrqd', p_w.astype(v_b.dtype), v_b)
        return g_b[..., 0:1] * o_c + g_b[..., 1:2] * o_s + g_b[..., 2:3] * o_w

    n_chunks = S // QB
    out = lax.map(block, (jnp.arange(n_chunks), chunk_seq(q, 3, QB), chunk_seq(gates, 3, QB)))
    out = unchunk_seq(out, 3).reshape(B, NSA_HEADS, S, D)
    return merge_heads(out)

def dilated_attention(q, k, v, q_norm):
    B, S, _ = q.shape
    H, D, QB = DIL_SLOTS, HEAD_DIM, DIL_Q_BLOCK
    scale = D ** -0.5
    q = q.reshape(B, S, N_DIL_GROUPS, H, D).transpose(0, 2, 3, 1, 4)
    q = rope(rmsnorm(q, q_norm[:, None, None, :]), jnp.arange(S))

    def block(args):
        c, q_b = args
        t = c * QB + jnp.arange(QB)
        outs, lses = [], []
        for gi, (window, dil) in enumerate(DIL_PATTERNS):
            n_k = window // dil + 1
            idx = t[:, None] - dil * jnp.arange(n_k)[None, :]
            valid = idx >= 0
            idx = jnp.maximum(idx, 0)
            k_g = jnp.take(k, idx, axis=2)
            v_g = jnp.take(v, idx, axis=2)
            s = jnp.einsum('bhqd,bhqkd->bhqk', q_b[:, gi], k_g).astype(jnp.float32) * scale
            s = jnp.where(valid, s, NEG)
            lse = jax.nn.logsumexp(s, axis=-1, keepdims=True)
            p = jnp.exp(s - lse)
            outs.append(jnp.einsum('bhqk,bhqkd->bhqd', p.astype(v.dtype), v_g))
            lses.append(lse)
        wts = jax.nn.softmax(jnp.stack(lses), axis=0).astype(v.dtype)
        return jnp.sum(jnp.stack(outs) * wts, axis=0)

    out = lax.map(block, (jnp.arange(S // QB), chunk_seq(q, 3, QB)))
    return merge_heads(unchunk_seq(out, 2))

def memory_attention(q, mem_kv, q_norm, k_norm):
    scale = HEAD_DIM ** -0.5
    q = rmsnorm(split_heads(q, MEM_HEADS), q_norm)
    k, v = jnp.split(mem_kv, 2, axis=-1)
    k = rmsnorm(split_heads(k, MEM_HEADS), k_norm)
    v = split_heads(v, MEM_HEADS)
    p = jax.nn.softmax(jnp.einsum('bhqd,bhmd->bhqm', q, k).astype(jnp.float32) * scale, axis=-1)
    return merge_heads(jnp.einsum('bhqm,bhmd->bhqd', p.astype(v.dtype), v))

def squared_relu_mlp(h, w_up, w_down):
    return jnp.square(jax.nn.relu(h @ w_up)) @ w_down

def second_inputs(seed: int = 0) -> dict:
    key = jax.random.key(seed)
    keys = jax.random.split(key, 25)
    cnt = [0]

    def nk():
        k = keys[cnt[0]]
        cnt[0] += 1
        return k

    def normal(shape, scale):
        return scale * jax.random.normal(nk(), shape, jnp.float32)

    def gain(shape):
        return 1.0 + 0.05 * jax.random.normal(nk(), shape, jnp.float32)

    NA, NB = N_A_LAYERS, N_B_LAYERS
    return {
        "x": normal((BATCH, SEQ, D_MODEL), 1.0),
        "mem": normal((BATCH, N_MEM, D_MODEL), 1.0),
        "attn_norm": gain((DEPTH, D_MODEL)),
        "mlp_norm": gain((DEPTH, D_MODEL)),
        "w_up": normal((DEPTH, D_MODEL, D_FF_2), D_MODEL ** -0.5),
        "w_down": normal((DEPTH, D_FF_2, D_MODEL), D_FF_2 ** -0.5),
        "mem_norm": gain((DEPTH, D_MODEL)),
        "w_mem_kv": normal((DEPTH, D_MODEL, 2 * MEM_W), D_MODEL ** -0.5),
        "mem_q_norm": gain((DEPTH, HEAD_DIM)),
        "mem_k_norm": gain((DEPTH, HEAD_DIM)),
        "a_w_in": normal((NA, D_MODEL, A_IN), D_MODEL ** -0.5),
        "a_w_out": normal((NA, A_OUT, D_MODEL), A_OUT ** -0.5),
        "a_q_norm": gain((NA, HEAD_DIM)),
        "a_k_norm": gain((NA, 3, HEAD_DIM)),
        "a_cmp_pos": normal((NA, 2, CMP_BLOCK, HEAD_DIM), 0.1),
        "a_cmp_w1": normal((NA, 2, CMP_BLOCK * HEAD_DIM, CMP_HIDDEN), (CMP_BLOCK * HEAD_DIM) ** -0.5),
        "a_cmp_b1": normal((NA, 2, CMP_HIDDEN), 0.01),
        "a_cmp_w2": normal((NA, 2, CMP_HIDDEN, HEAD_DIM), CMP_HIDDEN ** -0.5),
        "a_cmp_b2": normal((NA, 2, HEAD_DIM), 0.01),
        "kv_norm": gain((D_MODEL,)),
        "w_kv_shared": normal((D_MODEL, SHARED_KV), D_MODEL ** -0.5),
        "kv_k_norm": gain((HEAD_DIM,)),
        "b_w_in": normal((NB, D_MODEL, B_IN), D_MODEL ** -0.5),
        "b_w_out": normal((NB, B_OUT, D_MODEL), B_OUT ** -0.5),
        "b_q_norm": gain((NB, N_DIL_GROUPS, HEAD_DIM)),
    }

def second_block(x, mem, attn_norm, mlp_norm, w_up, w_down, mem_norm, w_mem_kv, mem_q_norm, mem_k_norm,
              a_w_in, a_w_out, a_q_norm, a_k_norm, a_cmp_pos, a_cmp_w1, a_cmp_b1, a_cmp_w2, a_cmp_b2,
              kv_norm, w_kv_shared, kv_k_norm, b_w_in, b_w_out, b_q_norm):
    pos = jnp.arange(x.shape[1])
    k_shared = None
    v_shared = None
    for layer in range(DEPTH):
        h = rmsnorm(x, attn_norm[layer])
        mem_kv = rmsnorm(mem, mem_norm[layer]) @ w_mem_kv[layer]
        if layer < N_A_LAYERS:
            i = layer
            q, kc, vc, ks, vs, kw, vw, q_mem, gl = jnp.split(h @ a_w_in[i], A_SPLITS, axis=-1)
            o_main = nsa_attention(q, kc, vc, ks, vs, kw, vw, gl, a_q_norm[i], a_k_norm[i],
                                   a_cmp_pos[i], a_cmp_w1[i], a_cmp_b1[i], a_cmp_w2[i], a_cmp_b2[i])
            o_mem = memory_attention(q_mem, mem_kv, mem_q_norm[layer], mem_k_norm[layer])
            x = x + jnp.concatenate([o_main, o_mem], axis=-1) @ a_w_out[i]
        else:
            i = layer - N_A_LAYERS
            if i == 0:
                k_s, v_s = jnp.split(rmsnorm(x, kv_norm) @ w_kv_shared, 2, axis=-1)
                k_shared = rope(rmsnorm(split_heads(k_s, DIL_SLOTS), kv_k_norm), pos)
                v_shared = split_heads(v_s, DIL_SLOTS)
            q, q_mem = jnp.split(h @ b_w_in[i], [B_Q], axis=-1)
            o_main = dilated_attention(q, k_shared, v_shared, b_q_norm[i])
            o_mem = memory_attention(q_mem, mem_kv, mem_q_norm[layer], mem_k_norm[layer])
            x = x + jnp.concatenate([o_main, o_mem], axis=-1) @ b_w_out[i]
        x = x + squared_relu_mlp(rmsnorm(x, mlp_norm[layer]), w_up[layer], w_down[layer])
    return x


def setup_inputs(seed=0):
    out = dict(first_inputs(seed))
    for name, value in second_inputs(seed + 1).items():
        if name != "x":
            out[name + "_2"] = value
    return out


def reference(
    x, c, ctx, c_ctx, norm_g, ada_w, ada_b, ffn_w1, ffn_w3, ffn_w2, ab_w_in, ab_a_qn, ab_a_kn,
    ab_b_qn, ab_b_kn, ab_b_kvn, ab_b_wukv, ab_w_out, cd_w_in, hgrn_lb, cd_c_gn, cd_d_qn,
    cd_d_kn, cd_d_rpb, cd_w_out, mem_2, attn_norm_2, mlp_norm_2, w_up_2, w_down_2, mem_norm_2,
    w_mem_kv_2, mem_q_norm_2, mem_k_norm_2, a_w_in_2, a_w_out_2, a_q_norm_2, a_k_norm_2,
    a_cmp_pos_2, a_cmp_w1_2, a_cmp_b1_2, a_cmp_w2_2, a_cmp_b2_2, kv_norm_2, w_kv_shared_2,
    kv_k_norm_2, b_w_in_2, b_w_out_2, b_q_norm_2,
):
    x = first_block(
        x, c, ctx, c_ctx, norm_g, ada_w, ada_b, ffn_w1, ffn_w3, ffn_w2, ab_w_in, ab_a_qn,
        ab_a_kn, ab_b_qn, ab_b_kn, ab_b_kvn, ab_b_wukv, ab_w_out, cd_w_in, hgrn_lb, cd_c_gn,
        cd_d_qn, cd_d_kn, cd_d_rpb, cd_w_out,
    )
    return second_block(
        x, mem_2, attn_norm_2, mlp_norm_2, w_up_2, w_down_2, mem_norm_2, w_mem_kv_2,
        mem_q_norm_2, mem_k_norm_2, a_w_in_2, a_w_out_2, a_q_norm_2, a_k_norm_2, a_cmp_pos_2,
        a_cmp_w1_2, a_cmp_b1_2, a_cmp_w2_2, a_cmp_b2_2, kv_norm_2, w_kv_shared_2, kv_k_norm_2,
        b_w_in_2, b_w_out_2, b_q_norm_2,
    )


_drawn_inputs = setup_inputs


def setup_inputs(seed=0):
    import zlib

    import numpy as np

    out = dict(_drawn_inputs(seed))
    spreads = {}
    factors = {'ab_a_qn': 8.0,
     'ab_a_kn': 8.0,
     'ab_b_qn': 8.0,
     'ab_b_kn': 8.0,
     'ab_b_kvn': 8.0,
     'hgrn_lb': 4.619,
     'cd_c_gn': 5.352,
     'cd_d_qn': 8.0,
     'cd_d_kn': 8.0,
     'cd_d_rpb': 7.249,
     'attn_norm_2': 3.184,
     'mem_norm_2': 8.0,
     'mem_q_norm_2': 8.0,
     'mem_k_norm_2': 8.0,
     'a_q_norm_2': 7.484,
     'a_k_norm_2': 8.0,
     'a_cmp_b1_2': 8.0,
     'a_cmp_b2_2': 8.0,
     'kv_norm_2': 4.622,
     'kv_k_norm_2': 8.0,
     'b_q_norm_2': 8.0}
    for name, (base, spread) in spreads.items():
        noise = np.random.default_rng([zlib.crc32(name.encode()), seed]).standard_normal(out[name].shape)
        drawn = base * np.exp(spread * noise) if base else spread * noise
        out[name] = jnp.asarray(drawn.astype(out[name].dtype))
    for name, factor in factors.items():
        out[name] = (out[name] * factor).astype(out[name].dtype)
    return out
```

```python
from contextlib import ExitStack, contextmanager

import numpy as np

import concourse.bass as bass
from concourse import mybir

F32 = mybir.dt.float32
ACT = mybir.ActivationFunctionType
ALU = mybir.AluOpType
AX = mybir.AxisListType.X
P = 128
CREDIT = 3
D = 1024
KD = D // P
SX = 256
SC = 256
TOK = SX + SC
DFF = 2816
KF = DFF // P
DFF2 = 4096
KF2 = DFF2 // P
EPS = 1e-6
NEG = -1e30
HD = 64
BQK = 96
GRID = 64
NCMP = 15
LEVELS = 7
LN_FLOOR = 2.0 ** -62
MODW = 9 * D
NADA = 2 * MODW // 512
ASLOTS = 4



def _rope_1d(pos, dim):
    inv = np.float32(10000.0) ** (-np.arange(0, dim, 2, dtype=np.float32) / np.float32(dim))
    ang = pos.astype(np.float32)[:, None] * inv[None, :].astype(np.float32)
    ang = np.concatenate([ang, ang], -1)
    return np.cos(ang), np.sin(ang)


def _axial(n, dim):
    t = np.arange(n)
    cr, sr = _rope_1d(t // GRID, dim // 2)
    cc, sc = _rope_1d(t % GRID, dim // 2)
    return np.concatenate([cr, cc], -1).T, np.concatenate([sr, sc], -1).T


def _rot(dim, half):
    m = np.zeros((dim, dim), np.float32)
    for d in range(dim):
        if d % (2 * half) < half:
            m[d + half, d] = -1.0
        else:
            m[d - half, d] = 1.0
    return m


def _blockdiag(*ms):
    n = sum(len(m) for m in ms)
    out = np.zeros((n, n), np.float32)
    at = 0
    for m in ms:
        out[at:at + len(m), at:at + len(m)] = m
        at += len(m)
    return out


def constants():
    c = {}
    f = np.float32
    c["ident"] = np.eye(P, dtype=f)
    c["ones"] = np.ones((P, P), f)
    c["turn"] = _blockdiag(np.eye(64, dtype=f)[::-1], np.eye(64, dtype=f)[::-1])
    c["ones64"] = _blockdiag(np.ones((64, 64), f), np.ones((64, 64), f))
    r64 = _rot(64, 16)
    c["rotA"] = _blockdiag(r64, r64)
    rb = np.zeros((P, P), f)
    rb[64:96, 64:96] = _rot(32, 8)
    c["rotB"] = rb
    rs = _rot(64, 32)
    c["rotS"] = _blockdiag(rs, rs)
    co, si = _axial(SX, 64)
    one, zero = np.ones((P, SC), f), np.zeros((P, SC), f)
    c["cosA"] = np.concatenate([np.concatenate([co, co], 0), one], 1)
    c["sinA"] = np.concatenate([np.concatenate([si, si], 0), zero], 1)
    cb, sb_ = _axial(SX, 32)
    cosb, sinb = np.ones((P, SX), f), np.zeros((P, SX), f)
    cosb[64:96], sinb[64:96] = cb, sb_
    c["cosB"] = np.concatenate([cosb, one], 1)
    c["sinB"] = np.concatenate([sinb, zero], 1)
    cs, ss = _rope_1d(np.arange(SX), 64)
    c["cosS"] = np.concatenate([cs.T, cs.T], 0)
    c["sinS"] = np.concatenate([ss.T, ss.T], 0)
    ce, se = _rope_1d(np.arange(NCMP) * 16 + 31, 64)
    c["cosC"] = np.tile(np.concatenate([ce.T, ce.T], 0), (1, 3))
    c["sinC"] = np.tile(np.concatenate([se.T, se.T], 0), (1, 3))
    t = np.arange(SX)[:, None]
    s = np.arange(SX)[None, :]
    add = lambda ok: np.where(ok, 0.0, NEG).astype(f)
    causal = s <= t
    cmp_ok = (np.arange(NCMP)[None, :] * 16 + 31) <= t
    nsa = np.concatenate([add(causal), add(causal), add(cmp_ok)], 1)
    dil = np.concatenate([add(causal & (t - s <= 128)), add(causal & ((t - s) % 4 == 0)),
                          add(causal & ((t - s) % 16 == 0))], 1)
    for tb in range(2):
        c[f"nsa{tb}"] = nsa[tb * P:(tb + 1) * P]
        c[f"dil{tb}"] = dil[tb * P:(tb + 1) * P]
    c["cmpany"] = np.stack([cmp_ok[:P].any(1), cmp_ok[P:].any(1)], 1).astype(f)
    col = np.arange(P) % GRID
    start = np.clip(col - 8, 0, GRID - 16)[:, None]
    kc = np.arange(GRID)[None, :]
    c["window"] = np.tile(add((kc >= start) & (kc < start + 16)), (1, 4))
    for way in range(2):
        flip = (lambda m: m[::-1, ::-1]) if way else (lambda m: m)
        sums, masks = [], []
        u = np.arange(P)[:, None]
        v = np.arange(P)[None, :]
        for lev in range(LEVELS):
            half = 64 >> lev
            b = (v // (2 * half)) * 2 * half + half
            right = v >= b
            sums.append(flip(np.where(right, (u >= b) & (u <= v), (u > v) & (u < b)).astype(f)))
            bu = (u // (2 * half)) * 2 * half + half
            masks.append(flip(((u < bu) & (v >= bu) & (u // (2 * half) == v // (2 * half))).astype(f)))
        masks.append(np.eye(P, dtype=f))
        sums.append(flip((u <= v).astype(f)))
        sums.append(np.ones((P, 1), f))
        c[f"sums{way}"] = np.concatenate(sums, 1)
        c[f"hmask{way}"] = np.concatenate(masks, 1)
        c[f"after{way}"] = flip((u > v).astype(f))
    return c


def pack(tables):
    where, at = {}, 0
    for k, v in tables.items():
        where[k] = (at, v.shape[1])
        at += v.shape[1]
    return where, np.ascontiguousarray(np.concatenate([v.astype(np.float32) for v in tables.values()], 1))




def col(v):
    v = np.asarray(v)
    return v.reshape(-1, P).T


def dup(v):
    return np.concatenate([np.asarray(v).reshape(64), np.asarray(v).reshape(64)]).reshape(P, 1)


def pad(v):
    v = np.asarray(v).reshape(-1, 1)
    return np.concatenate([v, np.zeros((P - len(v), 1), v.dtype)])


def beside(*columns):
    return np.concatenate([np.repeat(v, n, 1) for v, n in columns], 1)


def tiles(*ws):
    out = [np.asarray(w).reshape(w.shape[0] // P, P, -1, P).transpose(1, 2, 0, 3) for w in ws]
    n = out[0].shape[1]
    return np.ascontiguousarray(np.stack(out, 2)).reshape(P, n, -1)


def rows(w):
    w = np.asarray(w)
    return np.ascontiguousarray(w.reshape(w.shape[0] // P, P, -1).transpose(1, 0, 2)).reshape(P, -1)


def tiles96(w):
    w = np.asarray(w)
    return np.ascontiguousarray(w.reshape(w.shape[0] // P, P, -1, 96).transpose(1, 2, 0, 3)).reshape(P, -1, w.shape[0] // P * 96)


A_PAIRS = [h for j in range(4) for h in (j, j + 4)]
S_PAIRS = [h for j in range(4) for h in (j, j + 4)] + [8, 9, 10, 11]
S_KV = [0, 1, 2, 2]


def heads(w, order, axis, width=HD):
    w = np.asarray(w)
    shape = w.shape[:axis] + (w.shape[axis] // width, width) + w.shape[axis + 1:]
    return np.take(w.reshape(shape), order, axis=axis).reshape(
        w.shape[:axis] + (len(order) * width,) + w.shape[axis + 1:])


def layout(i):
    i = {k: np.asarray(v) for k, v in i.items()}
    a = {}
    fm = lambda x: np.ascontiguousarray(x.T.reshape(KD, P, -1).transpose(1, 0, 2))
    a["x"] = fm(np.concatenate([i["x"][0], i["ctx"][0]], 0))
    a["mem"] = fm(i["mem_2"][0])
    a["ada"] = np.ascontiguousarray(
        i["ada_w"].reshape(2, KD, P, MODW // 512, 512).transpose(2, 0, 3, 1, 4)).reshape(P, NADA, KD * 512)
    for l in range(2):
        for f in range(2):
            a[f"ff1_{l}{f}"] = tiles(i["ffn_w1"][l, f], i["ffn_w3"][l, f])
            a[f"ff2_{l}{f}"] = tiles(i["ffn_w2"][l, f])
        a[f"up{l}"] = tiles(i["w_up_2"][l])
        a[f"down{l}"] = tiles(i["w_down_2"][l])
        a[f"memk{l}"] = tiles(i["w_mem_kv_2"][l][:, :256])
        a[f"memv{l}"] = rows(i["w_mem_kv_2"][l][:, 256:])
    w = i["ab_w_in"][0]
    a["ab_q"] = tiles(np.concatenate([heads(w[:, :512], A_PAIRS, 1), w[:, 512:640]], 1))
    a["ab_v"] = rows(w[:, 640:768])
    a["ab_bq"] = tiles96(w[:, 768:1536])
    a["ab_bkv"] = tiles(w[:, 1536:1792])
    a["ab_bkr"] = tiles96(w[:, 1728:1824])
    u = i["ab_b_wukv"][0].reshape(256, 8, 128)
    a["ab_ukn"] = np.ascontiguousarray(u[:, :, :64].reshape(2, P, 8, 64).transpose(1, 2, 0, 3)).reshape(P, 8, 128)
    a["ab_ukv"] = np.ascontiguousarray(u[:, :, 64:].reshape(2, P, 512).transpose(1, 0, 2)).reshape(P, 1024)
    w = i["ab_w_out"][0]
    a["ab_out"] = tiles(np.concatenate([heads(w[:512], A_PAIRS, 0), w[512:]], 0))
    w = i["cd_w_in"][0]
    a["cd_q"] = tiles(w[:, :512])
    a["cd_rows"] = np.ascontiguousarray(np.stack(
        [rows(w[:, n:n + 512]) for n in (512, 1024, 1536, 3584, 2048)], 1))
    a["cd_dq"] = tiles(w[:, 2560:3072])
    a["cd_dk"] = tiles(w[:, 3072:3584])
    a["cd_out"] = tiles(i["cd_w_out"][0])
    a["lb"] = i["hgrn_lb"].reshape(2, 1024)
    a["rpb"] = i["cd_d_rpb"][0].reshape(-1)
    a["c_gn"] = i["cd_c_gn"]
    w = i["a_w_in_2"][0]
    cut = lambda n, m: w[:, n:n + m]
    a["s_q"] = tiles(np.concatenate([heads(cut(0, 768), S_PAIRS, 1), heads(cut(1152, 192), S_KV, 1),
                                     heads(cut(1536, 192), S_KV, 1), cut(1920, 256)], 1))
    a["s_cmp"] = tiles(heads(cut(768, 384), [0, 0, 1, 1, 2, 2, 3, 3, 4, 4, 5, 5], 1))
    gates = cut(2176, 36).reshape(D, 12, 3)[:, S_PAIRS][:, :, [1, 2, 0]].reshape(D, 36)
    a["s_v"] = rows(np.concatenate([heads(cut(1344, 192), S_KV, 1), heads(cut(1728, 192), S_KV, 1)], 1))
    a["s_g"] = rows(gates)
    a["s_w1"] = np.ascontiguousarray(np.stack([tiles(i["a_cmp_w1_2"][0, n]) for n in range(2)], 1))
    w2 = i["a_cmp_w2_2"][0]
    a["s_w2"] = np.ascontiguousarray(np.concatenate(
        [rows(np.concatenate([w2[0], w2[0]], 1)), rows(w2[1])], 1))
    a["s_b2v"] = i["a_cmp_b2_2"][0, 1:2]
    w = i["a_w_out_2"][0]
    a["s_out"] = tiles(np.concatenate([heads(w[:768], S_PAIRS, 0), w[768:]], 0))
    a["d_k"] = tiles(i["w_kv_shared_2"][:, :512])
    a["d_v"] = rows(i["w_kv_shared_2"][:, 512:])
    a["d_q"] = tiles(i["b_w_in_2"][0])
    a["d_out"] = tiles(i["b_w_out_2"][0])
    v = {
        "c": np.stack([col(i["c"][0]), col(i["c_ctx"])], 2).reshape(P, 2 * KD),
        "norm_g": col(i["norm_g"]),
        "ada_b": col(i["ada_b"]),
        "attn_norm": col(i["attn_norm_2"]), "mlp_norm": col(i["mlp_norm_2"]),
        "mem_norm": col(i["mem_norm_2"]), "kv_norm": col(i["kv_norm_2"]),
        "b_kvn": col(i["ab_b_kvn"][0]),
        "gain_a": beside((dup(i["ab_a_qn"][0]), 4), (dup(i["ab_a_kn"][0]), 1)),
        "gain_b": beside((pad(i["ab_b_qn"][0]), 8), (pad(i["ab_b_kn"][0]), 8)),
        "gain_d": beside((dup(i["cd_d_qn"][0]), 4), (dup(i["cd_d_kn"][0]), 4)),
        "gain_s": beside((dup(i["a_q_norm_2"][0]), 6), *[(dup(i["a_k_norm_2"][0, n]), 2) for n in (1, 2)]),
        "gain_c": dup(i["a_k_norm_2"][0, 0]),
        "gain_g": beside((dup(i["kv_k_norm_2"]), 4), *[(dup(i["b_q_norm_2"][0, n]), 4) for n in range(3)]),
        **{f"gain_m{l}": beside((dup(i["mem_q_norm_2"][l]), 2), (dup(i["mem_k_norm_2"][l]), 2)) for l in range(2)},
        "cmp_pos": i["a_cmp_pos_2"][0].reshape(2, 16, P).transpose(2, 0, 1).reshape(P, 32),
        "cmp_b1": col(i["a_cmp_b1_2"][0]),
        "cmp_b2": dup(i["a_cmp_b2_2"][0, 0]),
    }
    v_at, a["vectors"] = pack(v)
    c_at, a["tables"] = pack(constants())
    return a, v_at, c_at




class Counter:

    def __init__(self, sem, credit=CREDIT):
        self.sem, self.base = sem, credit

    def at(self, k):
        return self.base + k

    def passed(self, k):
        self.base += k


class Steps:

    def __init__(self, eng, counter):
        self.eng, self.counter, self.start, self.k, self.off = eng, counter, 0, 0, 0

    def then(self, ins):
        ins.then_inc(self.counter.sem, 1)
        self.k += 1
        self.eng.wait_ge(self.counter.sem, self.counter.at(self.off + self.k))

    def iteration(self, n, per):
        self.off, self.k = self.start + n * per, 0

    def iterated(self, n, per):
        assert self.k == per, f"{self.k} steps in an iteration, not {per}"
        self.start += n * per
        self.off, self.k = self.start, 0

    def done(self):
        return self.start + self.k


def pairs(eng, n, body, first=0, steps=None, per=0, start=0):
    if n // 2 > start:
        with eng.Fori(start, n // 2) as i:
            if steps is not None:
                steps.iteration(i, 2 * per)
            body([(i * 2 + s, i * 2 + (first + s), (first + s) % 2, i + ((first + s) // 2 + 1)) for s in range(2)])
        if steps is not None:
            steps.iterated(n // 2, 2 * per)
    if n % 2:
        g = first + n - 1
        if steps is not None:
            steps.iteration(0, per)
        body([(n - 1, g, g % 2, g // 2 + 1)])
        if steps is not None:
            steps.iterated(1, per)


def each(eng, n, body, first=0, steps=None, per=0, start=0):
    def both(ts):
        for t in ts:
            body(*t)
    pairs(eng, n, both, first, steps, per, start)


class Core:

    def __init__(self, nc, ctx, args, v_at, c_at):
        self.nc, self.a, self.v_at, self.c_at = nc, args, v_at, c_at
        sb = lambda n, shape: ctx.enter_context(nc.sbuf_tensor(n, shape, F32))
        self.x = sb("x_fm", [P, KD, TOK])
        self.h = sb("h_fm", [P, KD, TOK])
        self.arena = sb("arena", [P, 18432])
        self.w = sb("weights", [P, 2, 4096])
        self.pt = sb("probs_t", [P, 4096])
        self.tab = sb("tables_sb", [P, args["tables"].shape[1]])
        self.vec = sb("vectors_sb", [P, args["vectors"].shape[1]])
        self.mod = sb("mods", [P, 2, 9, KD, 2])
        self.small = sb("small", [P, 256])
        self.ps = ctx.enter_context(nc.psum_tensor("ps", [P, 8, 512], F32))
        self.counters = []

        def counter(name):
            self.counters.append(Counter(ctx.enter_context(nc.semaphore(name))))
            return self.counters[-1]
        self.psum_free = counter("psum_free")
        self.tile_done = counter("tile_done")
        self.silu_ready = counter("silu_ready")
        self.square_ready = counter("square_ready")
        self.stat_ready = counter("stat_ready")
        self.rinv_ready = counter("rinv_ready")
        self.rot_ready = counter("rot_ready")
        self.normed_ready = counter("normed_ready")
        self.rotated = counter("rotated")
        self.dve_step = counter("dve_step")
        self.act_step = counter("act_step")
        self.pool_step = counter("pool_step")
        self.q_staged = counter("q_staged")
        self.turns = counter("turns")
        self.scores_done = counter("scores_done")
        self.max_ready = counter("max_ready")
        self.exp_done = counter("exp_done")
        self.p_ready = counter("p_ready")
        self.pt_done = counter("pt_done")
        self.pt_copied = counter("pt_copied")
        self.heads_done = counter("heads_done")
        self.o_copied = counter("o_copied")
        self.ready_a = counter("ready_a")
        self.ready_b = counter("ready_b")
        self.ready_c = counter("ready_c")
        self.ready_d = counter("ready_d")
        self.ready_e = counter("ready_e")
        self.loaded = [Counter(ctx.enter_context(nc.semaphore(f"loaded{s}")), 0) for s in range(ASLOTS)]
        self.x_loaded = Counter(ctx.enter_context(nc.semaphore("x_loaded")), 0)
        self.fetched = Counter(ctx.enter_context(nc.semaphore("fetched")), 0)
        self.stored = Counter(ctx.enter_context(nc.semaphore("stored")), 0)

    def v(self, name, i=0, n=1):
        at = self.v_at[name][0]
        return self.vec[:, at + i:at + i + n]

    def t(self, name):
        at, n = self.c_at[name]
        return self.tab[:, at:at + n]

    def region(self, at, *dims):
        n = int(np.prod(dims))
        assert at + n <= 18432
        flat = self.arena[:, at:at + n]
        return split(flat, *dims)


LN_EXP_SET = 6


def load_ln_exp(nc, act):
    act.add_instruction(mybir.InstLoadActFuncSet(act_func_set_id=LN_EXP_SET, name=nc.get_next_instruction_name(),
                                                 engine=mybir.EngineType.Activation, ins=[], outs=[]))


def split(flat, *dims):
    if len(dims) == 2:
        return flat.rearrange("p (a b) -> p a b", a=dims[0])
    if len(dims) == 3:
        return flat.rearrange("p (a b c) -> p a b c", a=dims[0], b=dims[1])
    return flat




def one(ap, i):
    return ap[:, bass.ds(i, 1)]


class Dense:

    def __init__(self, w, n, kt, rhs, tok, vector=None, scalar=None, groups=1, m=P, free="vector", steps=0,
                 after=False):
        self.after = after
        self.w, self.n, self.kt, self.rhs, self.tok = w, n, kt, rhs, tok
        self.vector, self.scalar, self.groups, self.m = vector, scalar, groups, m
        self.free, self.steps = free, steps


def load_ahead(core, sp, job):
    for slot in range(2):
        sp.dma_start(core.w[:, slot, 0:job.groups * job.kt * job.m], job.w[:, slot]).then_inc(core.loaded[slot].sem, 16)


def dense_stage(core, *jobs, ahead=False):
    c, nc = core, core.nc
    total = sum(j.n for j in jobs)
    with nc.Block(no_gpsimd_drain=True) as block:

        @block.sync
        def _(sp):
            first = 0
            for j in jobs:
                size = j.groups * j.kt * j.m

                def load(t, g, slot, nth, j=j, size=size):
                    sp.wait_ge(c.tile_done.sem, c.tile_done.at(g - 1))
                    sp.dma_start(c.w[:, slot, 0:size], one(j.w, t)).then_inc(c.loaded[slot].sem, 16)
                each(sp, j.n, load, first, start=int(ahead and first == 0))
                first += j.n

        @block.tensor
        def _(pe):
            first = 0
            for j in jobs:
                if j.after:
                    pe.wait_ge(c.psum_free.sem, c.psum_free.at(first))
                def multiply(t, g, slot, nth, j=j):
                    pe.wait_ge(c.loaded[slot].sem, c.loaded[slot].at(nth * 16))
                    pe.wait_ge(c.psum_free.sem, c.psum_free.at(g - 1))
                    for a in range(j.groups):
                        for k in range(j.kt):
                            w = c.w[:, slot, (a * j.kt + k) * j.m:(a * j.kt + k + 1) * j.m]
                            last = pe.matmul(c.ps[0:j.m, slot * 2 + a, 0:j.tok], w, j.rhs[:, k, 0:j.tok],
                                             start=(k == 0), stop=(k == j.kt - 1))
                    last.then_inc(c.tile_done.sem, 1)
                each(pe, j.n, multiply, first)
                first += j.n

        @block.scalar
        def _(act):
            first = 0
            for j in jobs:
                if j.scalar:
                    def take(t, g, slot, nth, j=j):
                        act.wait_ge(c.tile_done.sem, c.tile_done.at(g + 1))
                        last = j.scalar(act, t, g, slot, [c.ps[0:j.m, slot * 2 + a, 0:j.tok] for a in range(j.groups)])
                        if j.free == "scalar":
                            last.then_inc(c.psum_free.sem, 1)
                    each(act, j.n, take, first)
                first += j.n

        @block.vector
        def _(dv):
            first, steps = 0, Steps(dv, c.dve_step)
            for j in jobs:
                if j.vector:
                    def take(t, g, slot, nth, j=j):
                        dv.wait_ge(c.tile_done.sem, c.tile_done.at(g + 1))
                        last = j.vector(dv, t, g, slot, [c.ps[0:j.m, slot * 2 + a, 0:j.tok] for a in range(j.groups)], steps)
                        if j.free == "vector":
                            last.then_inc(c.psum_free.sem, 1)
                    each(dv, j.n, take, first, steps, j.steps)
                first += j.n
            c.dve_step.passed(steps.done())
    c.tile_done.passed(total)
    c.psum_free.passed(total)
    c.silu_ready.passed(sum(j.n for j in jobs if j.scalar and j.vector))
    for s in range(2):
        c.loaded[s].passed(16 * ((total + 1 - s) // 2))






def load_stage(core):
    c, nc, a = core, core.nc, core.a
    with nc.Block(no_gpsimd_drain=True) as block:

        @block.sync
        def _(sp):
            sp.dma_start(c.vec[:], a["vectors"]).then_inc(c.fetched.sem, 16)
            sp.dma_start(c.tab[:, 0:P], a["tables"][:, 0:P]).then_inc(c.fetched.sem, 16)
            for t in range(ASLOTS):
                sp.dma_start(c.region(t * 4096, 4096), a["ada"][:, t]).then_inc(c.loaded[t].sem, 16)

        @block.gpsimd
        def _(pool):
            for n in c.counters:
                pool.sem_inc(n.sem, CREDIT)


def ada_stage(core):
    c, nc = core, core.nc
    cs = c.small[:, 0:2 * KD]
    row = split(c.pt[0:2, 0:1024], 2, 512)
    weights = c.region(0, ASLOTS, 4096)
    mods = c.mod[:].rearrange("p l m k t -> p (l m k) t")
    bias = c.v("ada_b", 0, 144)
    rounds = NADA // ASLOTS

    def loop(eng, body, start=0):
        with eng.Fori(start, rounds) as i:
            body(i, [(a, i * ASLOTS + a) for a in range(ASLOTS)])
    with nc.Block(no_gpsimd_drain=True) as block:

        @block.sync
        def _(sp):
            def load(i, ts):
                for a, t in ts:
                    sp.wait_ge(c.tile_done.sem, c.tile_done.at(t - (ASLOTS - 1)))
                    sp.dma_start(weights[:, a], one(c.a["ada"], t)).then_inc(c.loaded[a].sem, 16)
            loop(sp, load, 1)
            sp.dma_start(c.tab[:, P:], c.a["tables"][:, P:]).then_inc(c.x_loaded.sem, 16)
            sp.dma_start(c.x[:], c.a["x"]).then_inc(c.x_loaded.sem, 16)

        @block.scalar
        def _(act):
            act.wait_ge(c.fetched.sem, c.fetched.at(32))
            act.activation(cs, c.v("c", 0, 2 * KD), ACT.Silu).then_inc(c.silu_ready.sem, 1)

            def take(i, ts):
                for a, t in ts:
                    act.wait_ge(c.tile_done.sem, c.tile_done.at(t + 1))
                    act.wait_ge(c.ready_a.sem, c.ready_a.at(t - 1))
                    act.copy(row[:, a % 2], c.ps[0:2, a % 2, :]).then_inc(c.psum_free.sem, 1)
            loop(act, take)

        @block.tensor
        def _(pe):
            pe.wait_ge(c.silu_ready.sem, c.silu_ready.at(1))
            pe.wait_ge(c.fetched.sem, c.fetched.at(32))

            def multiply(i, a, t):
                pe.wait_ge(c.loaded[a].sem, c.loaded[a].at(i * 16 + 16))
                pe.wait_ge(c.psum_free.sem, c.psum_free.at(t - 1))
                for k in range(KD):
                    last = pe.matmul(c.ps[0:2, a % 2, :], cs[:, 2 * k:2 * k + 2],
                                     weights[:, a, k * 512:(k + 1) * 512], start=(k == 0), stop=(k == KD - 1))
                last.then_inc(c.tile_done.sem, 1)

            def turn(a, t):
                pe.wait_ge(c.psum_free.sem, c.psum_free.at(t + 1))
                pe.wait_ge(c.ready_b.sem, c.ready_b.at(t - 1))
                for b in range(4):
                    last = pe.matmul(c.ps[:, 2 + a % 2, 2 * b:2 * b + 2], row[:, a % 2, b * P:(b + 1) * P],
                                     c.t("ident")[0:2, 0:2], start=True, stop=True)
                last.then_inc(c.ready_a.sem, 1)

            def both(i, ts):
                for a, t in ts:
                    multiply(i, a, t)
                    if a:
                        turn(*ts[a - 1])
                turn(*ts[-1])
            loop(pe, both)

        @block.vector
        def _(dv):
            dv.wait_ge(c.fetched.sem, c.fetched.at(32))

            def take(i, ts):
                for a, t in ts:
                    dv.wait_ge(c.ready_a.sem, c.ready_a.at(t + 1))
                    src = c.ps[:, 2 + a % 2, 0:8].rearrange("p (b t) -> p b t", t=2)
                    for s in range(2):
                        last = dv.tensor_tensor(mods[:, bass.ds(t * 4, 4), s], src[:, :, s],
                                                bias[:, bass.ds(t * 4, 4)], ALU.add)
                    last.then_inc(c.ready_b.sem, 1)
            loop(dv, take)
            dv.wait_ge(c.x_loaded.sem, c.x_loaded.at(32))
    c.fetched.passed(32)
    for n in (c.tile_done, c.psum_free, c.ready_a, c.ready_b):
        n.passed(NADA)
    c.silu_ready.passed(1)
    for a in range(ASLOTS):
        c.loaded[a].passed(16 * rounds)


def gain_stage(core):
    c, nc = core, core.nc
    with nc.Block(no_gpsimd_drain=True) as block:

        @block.vector
        def _(dv):
            for l in range(2):
                for n, (scale, gate) in enumerate(((1, 2), (4, None), (7, 8))):
                    for s in range(2):
                        m = c.mod[:, l, scale, :, s]
                        dv.scalar_tensor_tensor(m, m, 1.0, c.v("norm_g", (l * 3 + n) * KD, KD), ALU.add, ALU.mult)
                    if gate:
                        dv.tensor_scalar(c.mod[:, l, gate], c.mod[:, l, gate], 0.5, None, ALU.mult)
            for n, lo, hi in (("gain_a", 0, 4), ("gain_b", 0, 8), ("gain_d", 0, 4), ("gain_s", 0, 6), ("gain_c", 0, 0),
                              ("gain_g", 4, 16), ("gain_m0", 0, 2), ("gain_m1", 0, 2)):
                d = BQK if n == "gain_b" else HD
                for first, end, scale in ((lo, hi, d ** -0.5), (0, lo, 1.0), (hi, c.v_at[n][1], 1.0)):
                    if end > first:
                        g = c.v(n, first, end - first)
                        dv.tensor_scalar(g, g, -0.5 / d * scale, None, ALU.mult)


def norm_stage(core, src, dst, kt, tok, gain, shift=None, scratch=None, then=None):
    c, nc = core, core.nc
    sq = dst if scratch is None else scratch
    rinv = c.pt[:, 0:tok]
    halves = [(0, 0, 256), (1, 256, 512)][:max(1, tok // 256)]
    with nc.Block(no_gpsimd_drain=True) as block:

        @block.sync
        def _(sp):
            if then:
                load_ahead(c, sp, then)

        @block.scalar
        def _(act):
            load_ln_exp(nc, act)
            for k in range(kt):
                act.activation(sq[:, k, 0:tok], src[:, k, 0:tok], ACT.Square).then_inc(c.square_ready.sem, 1)
            act.wait_ge(c.stat_ready.sem, c.stat_ready.at(1))
            act.activation(rinv, c.ps[:, 0, 0:tok], ACT.Ln, bias=EPS, scale=1.0 / (kt * P)).then_inc(c.act_step.sem, 1)
            act.wait_ge(c.act_step.sem, c.act_step.at(1))
            act.activation(rinv, rinv, ACT.Exp, scale=-0.5).then_inc(c.rinv_ready.sem, 1)
            if shift:
                for k in range(kt):
                    act.wait_ge(c.normed_ready.sem, c.normed_ready.at(k + 1))
                    for s, a, b in halves:
                        act.activation(dst[:, k, a:b], dst[:, k, a:b], ACT.Identity, bias=shift(k, s))

        @block.tensor
        def _(pe):
            for k in range(kt):
                pe.wait_ge(c.square_ready.sem, c.square_ready.at(k + 1))
                last = pe.matmul(c.ps[:, 0, 0:tok], c.t("ones"), sq[:, k, 0:tok], start=(k == 0), stop=(k == kt - 1))
            last.then_inc(c.stat_ready.sem, 1)

        @block.vector
        def _(dv):
            dv.wait_ge(c.rinv_ready.sem, c.rinv_ready.at(1))
            for k in range(kt):
                for s, a, b in halves:
                    last = dv.scalar_tensor_tensor(dst[:, k, a:b], src[:, k, a:b], gain(k, s), rinv[:, a:b],
                                                   ALU.mult, ALU.mult)
                last.then_inc(c.normed_ready.sem, 1)
    c.square_ready.passed(kt)
    c.normed_ready.passed(kt)
    for n in (c.act_step, c.stat_ready, c.rinv_ready):
        n.passed(1)




def mod_norm(core, l, n, tok, then):
    c = core
    norm_stage(c, c.x, c.h, KD, tok, lambda k, s: c.mod[:, l, 3 * n + 1, k, s:s + 1],
               lambda k, s: c.mod[:, l, 3 * n, k, s:s + 1], then=then)


def residual(core, l, gate, tok):
    c = core

    def take(dv, t, g, slot, banks, steps):
        for s in range(tok // 256):
            x = c.x[:, bass.ds(t, 1), s * 256:(s + 1) * 256]
            last = dv.scalar_tensor_tensor(x, split(banks[0][:, s * 256:(s + 1) * 256], 1, 256),
                                           c.mod[:, l, gate, bass.ds(t, 1), s:s + 1], x, ALU.mult, ALU.add)
        return last
    return take


def ffn(core, l, f, tok):
    c = core
    n = 0 if f == 0 else 2
    hidden = c.region(0, KF, 512)
    tmp = split(c.pt[:, 0:1024], 2, 512)

    def gate(act, t, g, slot, banks):
        act.wait_ge(c.psum_free.sem, c.psum_free.at(g - 1))
        return act.activation(tmp[:, slot, 0:tok], banks[0], ACT.Silu).then_inc(c.silu_ready.sem, 1)

    def product(dv, t, g, slot, banks, steps):
        dv.wait_ge(c.silu_ready.sem, c.silu_ready.at(g + 1))
        return dv.tensor_tensor(hidden[:, bass.ds(t, 1), 0:tok], split(tmp[:, slot, 0:tok], 1, tok),
                                split(banks[1], 1, tok), ALU.mult)
    up = Dense(c.a[f"ff1_{l}{f}"], KF, KD, c.h, tok, vector=product, scalar=gate, groups=2)
    down = Dense(c.a[f"ff2_{l}{f}"], KD, KF, hidden, tok, vector=residual(c, l, 3 * n + 2, tok), after=True)
    mod_norm(c, l, n, tok, up)
    dense_stage(c, up, down, ahead=True)





def rows_stage(core, kt, jobs):
    c, nc = core, core.nc
    work = [(j, b) for j, job in enumerate(jobs) for b in range(len(job[3]))]
    with nc.Block(no_gpsimd_drain=True) as block:

        @block.sync
        def _(sp):
            done = 0
            for j, (w, n, src, blocks, take) in enumerate(jobs):
                if j >= 2:
                    sp.wait_ge(c.tile_done.sem, c.tile_done.at(sum(len(x[3]) for x in jobs[:j - 1])))
                sp.dma_start(c.w[:, j % 2, 0:kt * n], w).then_inc(c.loaded[j % 2].sem, 16)

        @block.tensor
        def _(pe):
            for m, (j, b) in enumerate(work):
                w, n, src, blocks, take = jobs[j]
                pe.wait_ge(c.loaded[j % 2].sem, c.loaded[j % 2].at(16 * (j // 2 + 1)))
                pe.wait_ge(c.psum_free.sem, c.psum_free.at(m - 1))
                tb = blocks[b]
                for k in range(kt):
                    last = pe.matmul(c.ps[:, m % 2, 0:n], src[:, k, tb * P:(tb + 1) * P],
                                     c.w[:, j % 2, k * n:(k + 1) * n], start=(k == 0), stop=(k == kt - 1))
                last.then_inc(c.tile_done.sem, 1)

        @block.scalar
        def _(act):
            for m, (j, b) in enumerate(work):
                w, n, src, blocks, take = jobs[j]
                act.wait_ge(c.tile_done.sem, c.tile_done.at(m + 1))
                take(act, b, c.ps[:, m % 2, 0:n], m).then_inc(c.psum_free.sem, 1)
    c.tile_done.passed(len(work))
    c.psum_free.passed(len(work))
    for s in range(2):
        c.loaded[s].passed(16 * ((len(jobs) + 1 - s) // 2))




class Heads:

    def __init__(self, t, n, tok, ones, d, gains, rot=None, r=P):
        self.t, self.n, self.tok, self.ones, self.d, self.gains, self.rot, self.r = t, n, tok, ones, d, gains, rot, r


ROUND = 4


def heads_stage(core, *jobs):
    c, nc = core, core.nc
    turned = jobs[0].rot is not None
    assert all((j.rot is not None) == turned for j in jobs)
    total = sum(j.n for j in jobs)
    sq, y, cosine, sine = (split(c.pt[:, n * 1024:(n + 1) * 1024], 2, 512) for n in range(4))
    y2, newton = (split(c.w[:, 0, n * 1024:(n + 1) * 1024], 2, 512) for n in range(2))

    def over(eng, ops, steps=None, per=0):
        first = 0
        for j in jobs:
            def step(t, offset):
                for lag, what in ops:
                    if not isinstance(t, int) or 0 <= t - lag < j.n:
                        what(j, t - lag, t + (first - lag), (first + offset - lag) % 2)
            rounds = j.n // ROUND
            looped = rounds if rounds > 2 else 1
            for t in range(min(ROUND, j.n)):
                step(t, t)
            if looped > 1:
                if steps is not None:
                    steps.iterated(1, steps.k)
                with eng.Fori(1, looped) as i:
                    if steps is not None:
                        steps.iteration(i - 1, ROUND * per)
                    for o in range(ROUND):
                        step(i * ROUND + o, o)
                if steps is not None:
                    steps.iterated(looped - 1, ROUND * per)
            for t in range(looped * ROUND if j.n > ROUND else j.n, j.n + max(lag for lag, what in ops)):
                step(t, t)
            first += j.n

    def part(x, j, slot):
        return split(x[0:j.r, slot, 0:j.tok], 1, j.tok)
    with nc.Block(no_gpsimd_drain=True) as block:

        @block.scalar
        def _(act):
            load_ln_exp(nc, act)
            steps = Steps(act, c.act_step)

            def squares(j, t, g, slot):
                act.wait_ge(c.stat_ready.sem, c.stat_ready.at(g - 1))
                act.activation(part(sq, j, slot), one(j.t, t), ACT.Square).then_inc(c.square_ready.sem, 1)

            def roots(j, t, g, slot):
                act.wait_ge(c.stat_ready.sem, c.stat_ready.at(g + 1))
                act.wait_ge(c.normed_ready.sem, c.normed_ready.at(g - 1))
                r = part(y, j, slot)
                steps.then(act.activation(r, part(c.ps, j, slot), ACT.Ln, bias=EPS, scale=1.0 / j.d))
                steps.then(act.activation(r, r, ACT.Exp, scale=-0.5))
                act.activation(part(y2, j, slot), r, ACT.Square).then_inc(c.rinv_ready.sem, 1)

            def back(j, t, g, slot):
                act.wait_ge(c.rot_ready.sem, c.rot_ready.at(g + 1))
                act.sem_inc(c.turns.sem, 1)
                act.activation(one(j.t, t), part(c.ps, j, 2 + slot), ACT.Identity).then_inc(c.rotated.sem, 1)
            over(act, [(0, squares), (1, roots)] + [(3, back)] * turned, steps, 2)
            c.act_step.passed(steps.done())

        @block.tensor
        def _(pe):
            def stat(j, t, g, slot):
                pe.wait_ge(c.square_ready.sem, c.square_ready.at(g + 1))
                pe.wait_ge(c.normed_ready.sem, c.normed_ready.at(g - 1))
                pe.matmul(c.ps[0:j.r, slot, 0:j.tok], j.ones, sq[0:j.r, slot, 0:j.tok], start=True, stop=True)\
                  .then_inc(c.stat_ready.sem, 1)

            def rotate(j, t, g, slot):
                pe.wait_ge(c.ready_a.sem, c.ready_a.at(g + 1))
                pe.wait_ge(c.ready_b.sem, c.ready_b.at(g + 1))
                pe.wait_ge(c.rotated.sem, c.rotated.at(g - 1))
                bank = c.ps[0:j.r, 2 + slot, 0:j.tok]
                pe.matmul(bank, c.t("ident")[0:j.r, 0:j.r], cosine[0:j.r, slot, 0:j.tok], start=True, stop=False)
                pe.matmul(bank, j.rot[0], sine[0:j.r, slot, 0:j.tok], start=False, stop=True).then_inc(c.rot_ready.sem, 1)
            over(pe, [(0, stat)] + [(2, rotate)] * turned)

        @block.gpsimd
        def _(pool):
            def times_cosine(j, t, g, slot):
                pool.wait_ge(c.normed_ready.sem, c.normed_ready.at(g + 1))
                pool.wait_ge(c.rot_ready.sem, c.rot_ready.at(g - 1))
                pool.tensor_tensor(part(cosine, j, slot), one(j.t, t), split(j.rot[1], 1, j.tok), ALU.mult)\
                    .then_inc(c.ready_a.sem, 1)
            if turned:
                over(pool, [(0, times_cosine)])

        @block.vector
        def _(dv):
            steps = Steps(dv, c.dve_step)

            def norm(j, t, g, slot):
                dv.wait_ge(c.rinv_ready.sem, c.rinv_ready.at(g + 1))
                n = part(newton, j, slot)
                steps.then(dv.scalar_tensor_tensor(n, part(c.ps, j, slot), j.d * EPS, part(y2, j, slot), ALU.add, ALU.mult))
                steps.then(dv.scalar_tensor_tensor(n, n, -3.0 * j.d, part(y, j, slot), ALU.add, ALU.mult))
                dv.scalar_tensor_tensor(one(j.t, t), one(j.t, t), one(j.gains, t), n, ALU.mult, ALU.mult)\
                  .then_inc(c.normed_ready.sem, 1)

            def times_sine(j, t, g, slot):
                dv.wait_ge(c.normed_ready.sem, c.normed_ready.at(g + 1))
                dv.wait_ge(c.rot_ready.sem, c.rot_ready.at(g - 1))
                dv.tensor_tensor(part(sine, j, slot), one(j.t, t), split(j.rot[2], 1, j.tok), ALU.mult)\
                  .then_inc(c.ready_b.sem, 1)
            over(dv, [(0, norm)] + [(0, times_sine)] * turned, steps, 2)
            c.dve_step.passed(steps.done())
    for n in (c.square_ready, c.stat_ready, c.rinv_ready, c.normed_ready):
        n.passed(total)
    if turned:
        for n in (c.rot_ready, c.rotated, c.ready_a, c.ready_b):
            n.passed(total)




class Item:

    def __init__(self, s, tb, segs, soft, blocks, masks=(), fold=0):
        self.s, self.tb, self.segs, self.soft, self.blocks = s, tb, segs, soft, blocks
        self.masks, self.fold = masks, fold


def attention_stage(core, n, items, queries, values, out, tok, r=P):
    c, nc = core, core.nc
    ni = len(items)
    assert ni % 4 == 0 and n > 1
    flat = c.w[:].rearrange("p a b -> p (a b)")
    nq = len(queries)
    qs = split(flat[:, 0:nq * tok], nq, tok)
    nkb = 1 + max(b[2] for it in items for b in it.blocks)
    vs = split(flat[:, 2048:2048 + nkb * 128], nkb, 2, 64)
    probs = split(flat[:, 3072:3072 + 4096], 4, 1024)
    stat = flat[:, 7168:7168 + 64]
    pt = split(c.pt[:, 0:2 * nkb * P], 2, nkb, P)
    sc = c.ps[:, 0:4, :].rearrange("p (a b) n -> p a (b n)", a=2)
    copied = not callable(values)
    five = nkb == 5
    last_of = [max(m for m, it in enumerate(items) if it.s == s) for s in range(2)]
    first_of = [0, last_of[0] + 1]
    staging = [(kind, s, x) for s in range(2) for kind, xs in
               (("q", [(q, rows, src) for q, (hs, rows, src) in enumerate(queries) if hs == s]),
                ("v", [src for hs, src in values if hs == s] if copied else [])) for x in xs]
    copies = len(staging)

    def staged(kind, s):
        return max(k + 1 for k, (kd, hs, x) in enumerate(staging) if (kd, hs) == (kind, s))

    def small(kind, slot, b):
        return stat[:, (kind * 2 + slot) * 4 + b:(kind * 2 + slot) * 4 + b + 1]

    def pipeline(eng, ops, steps=None, per=0):
        def pair(i, first):
            for m in range(ni):
                for lag, what in ops:
                    if m >= lag:
                        what(i, m - lag)
                    elif not first:
                        what(i - 1, ni + m - lag)
        pair(0, True)
        if steps is not None:
            steps.iterated(1, steps.k)
        with eng.Fori(1, n) as i:
            if steps is not None:
                steps.iteration(i - 1, per)
            pair(i, False)
        if steps is not None:
            steps.iterated(n - 1, per)
        for m in range(max(lag for lag, what in ops)):
            for lag, what in ops:
                if lag > m:
                    what(n - 1, ni + m - lag)
    nlink = sum(len(it.masks) > 0 for it in items) + ni + sum(it.fold > 0 for it in items) * 2 \
        + sum(any(g for a, b, g in it.soft) for it in items)
    with nc.Block(no_gpsimd_drain=True) as block:

        @block.gpsimd
        def _(pool):
            steps = Steps(pool, c.pool_step)
            for q, (s, rows, src) in enumerate(queries):
                if rows is not None:
                    steps.then(pool.memset(qs[64 * (1 - s):64 * (1 - s) + 64, q, :], 0.0))
            c.pool_step.passed(steps.done())

            def stage(i, before):
                for k, (kind, s, x) in enumerate(staging):
                    if before is not None and kind == "q":
                        pool.wait_ge(c.scores_done.sem, c.scores_done.at(before * ni + last_of[s] + 1))
                    if before is not None and kind == "v":
                        pool.wait_ge(c.heads_done.sem, c.heads_done.at(before * ni + last_of[s] + 1))
                    if kind == "q":
                        q, rows, src = x
                        lo, hi = rows if rows is not None else (0, r)
                        copy = pool.tensor_copy(qs[lo:hi, q:q + 1, :], src(i))
                    else:
                        copy = pool.tensor_copy(vs[:, 0:nkb, s, :], x(i))
                    copy.then_inc(c.q_staged.sem, 1)
                    pool.wait_ge(c.q_staged.sem, c.q_staged.at(i * copies + k + 1))
            stage(0, None)
            with pool.Fori(1, n) as i:
                stage(i, i - 1)

        @block.tensor
        def _(pe):
            def scores(i, m):
                it = items[m]
                if m == first_of[it.s]:
                    pe.wait_ge(c.q_staged.sem, c.q_staged.at(i * copies + staged("q", it.s)))
                pe.wait_ge(c.exp_done.sem, c.exp_done.at(i * ni + (m - 1)))
                for a, w, q, keys in it.segs:
                    last = pe.matmul(sc[:, m % 2, a:a + w], qs[0:r, q, it.tb * P:(it.tb + 1) * P], keys(i),
                                     start=True, stop=True)
                last.then_inc(c.scores_done.sem, 1)

            def transposes(i, m):
                it = items[m]
                pe.wait_ge(c.p_ready.sem, c.p_ready.at(i * ni + m + 1))
                pe.wait_ge(c.pt_copied.sem, c.pt_copied.at(i * ni + (m if five else m - 1)))
                for a, w, b in it.blocks:
                    dst = c.ps[0:w, 4 + m % 2, b * P:(b + 1) * P] if b < 4 else c.ps[0:w, 7, 0:P]
                    last = pe.transpose(dst, probs[:, m % 4, a:a + w], c.t("ident"))
                last.then_inc(c.pt_done.sem, 1)

            def sums(i, m):
                it = items[m]
                s = it.s
                if m == first_of[s]:
                    if copied:
                        pe.wait_ge(c.q_staged.sem, c.q_staged.at(i * copies + staged("v", s)))
                    pe.wait_ge(c.o_copied.sem, c.o_copied.at(i * 2 + (s - 1)))
                pe.wait_ge(c.pt_copied.sem, c.pt_copied.at(i * ni + m + 1))
                for k, (a, w, b) in enumerate(it.blocks):
                    last = pe.matmul(c.ps[64 * s:64 * s + 64, 6, it.tb * P:(it.tb + 1) * P],
                                     vs[0:w, b, s, :] if copied else values(b, s), pt[0:w, m % 2, b, :],
                                     start=(k == 0), stop=(k == len(it.blocks) - 1))
                last.then_inc(c.heads_done.sem, 1)
            pipeline(pe, [(0, scores), (2, transposes), (3, sums)])

        @block.vector
        def _(dv):
            steps = Steps(dv, c.dve_step)

            def biggest(i, m):
                it = items[m]
                dv.wait_ge(c.scores_done.sem, c.scores_done.at(i * ni + m + 1))
                dv.wait_ge(c.pt_done.sem, c.pt_done.at(i * ni + (m - 2)))
                src = sc
                if it.masks:
                    for a, w, mask in it.masks:
                        if mask is None:
                            dv.tensor_copy(probs[:, m % 4, a:a + w], sc[:, m % 2, a:a + w])
                            continue
                        mk = mask(i)
                        shape = lambda x: split(x, mk.shape[1], mk.shape[2])
                        last = dv.tensor_tensor(shape(probs[:, m % 4, a:a + w]), shape(sc[:, m % 2, a:a + w]), mk, ALU.add)
                    steps.then(last)
                    src = probs
                for b, (a, e, gate) in enumerate(it.soft):
                    last = dv.tensor_reduce(small(0, m % 2, b), src[:, m % (4 if it.masks else 2), a:e], AX, ALU.max, negate=True)
                last.then_inc(c.max_ready.sem, 1)

            def norm(i, m):
                it = items[m]
                dv.wait_ge(c.exp_done.sem, c.exp_done.at(i * ni + m + 1))
                nb = len(it.soft)
                rec = stat[:, (4 + m % 2) * 4:(4 + m % 2) * 4 + nb]
                steps.then(dv.reciprocal(rec, stat[:, (2 + m % 2) * 4:(2 + m % 2) * 4 + nb]))
                if it.soft[0][2]:
                    steps.then(dv.tensor_tensor(rec, rec, it.soft[0][2](i), ALU.mult))
                if it.fold:
                    p = probs[:, m % 4, :]
                    w = it.fold
                    steps.then(dv.tensor_tensor(p[:, 0:w], p[:, 0:w], p[:, w:2 * w], ALU.add))
                    steps.then(dv.tensor_tensor(p[:, 0:w], p[:, 0:w], p[:, 2 * w:3 * w], ALU.add))
                for b, (a, e, gate) in enumerate(it.soft):
                    e = it.fold or e
                    last = dv.tensor_scalar(probs[:, m % 4, a:e], probs[:, m % 4, a:e], rec[:, b:b + 1], None, ALU.mult)
                last.then_inc(c.p_ready.sem, 1)

            def result(i, m):
                s = items[m].s
                if m == last_of[s]:
                    dv.wait_ge(c.heads_done.sem, c.heads_done.at(i * ni + m + 1))
                    r = slice(64 * s, 64 * s + 64)
                    dv.tensor_copy(out(i)[r], split(c.ps[r, 6, 0:tok], 1, tok)).then_inc(c.o_copied.sem, 1)
            pipeline(dv, [(0, biggest), (1, norm), (4, result)], steps, nlink)
            c.dve_step.passed(steps.done())

        @block.scalar
        def _(act):
            def expo(i, m):
                it = items[m]
                act.wait_ge(c.max_ready.sem, c.max_ready.at(i * ni + m + 1))
                src = probs if it.masks else sc
                if not it.masks:
                    act.wait_ge(c.pt_done.sem, c.pt_done.at(i * ni + (m - 2)))
                for b, (a, e, gate) in enumerate(it.soft):
                    last = act.activation(probs[:, m % 4, a:e], src[:, m % (4 if it.masks else 2), a:e], ACT.Exp,
                                          bias=small(0, m % 2, b), accum_out=small(1, m % 2, b))
                last.then_inc(c.exp_done.sem, 1)

            def back(i, m):
                it = items[m]
                act.wait_ge(c.pt_done.sem, c.pt_done.at(i * ni + m + 1))
                act.wait_ge(c.heads_done.sem, c.heads_done.at(i * ni + (m - 1)))
                full = [b for a, w, b in it.blocks if b < 4]
                for lo, hi in [(full[0], full[-1])] if full[-1] - full[0] == len(full) - 1 else [(b, b) for b in full]:
                    last = act.copy(pt[:, m % 2, lo:hi + 1, :],
                                    c.ps[:, 4 + m % 2, lo * P:(hi + 1) * P].rearrange("p (b t) -> p b t", t=P))
                if it.blocks[-1][2] == 4:
                    last = act.copy(pt[0:NCMP, m % 2, 4, :], c.ps[0:NCMP, 7, 0:P])
                last.then_inc(c.pt_copied.sem, 1)
            pipeline(act, [(0, expo), (2, back)])
    c.q_staged.passed(n * copies)
    for k in (c.scores_done, c.max_ready, c.exp_done, c.p_ready, c.pt_done, c.pt_copied, c.heads_done):
        k.passed(n * ni)
    c.o_copied.passed(2 * n)


def softmax_blocks(first, n):
    return [(b * P, P, first + b) for b in range(n)]




def copy_tile(dst, r=P):
    return lambda act, t, g, slot, banks: act.copy(dst[0:r, bass.ds(t, 1), :], banks[0].rearrange("p (a b) -> p a b", a=1))


def mixer_ab(core, stop):
    c = core
    qa, ka = c.region(0, 4, TOK), c.region(2048, 1, TOK)
    qka = c.region(0, 5, TOK)
    qb, kb = c.region(2560, 8, TOK), c.region(6656, 8, TOK)
    va, vb = c.region(10752, 4, 128), c.region(11264, 4, 512)
    bkv, bkr = c.region(13312, 2, TOK), c.region(14336, 1, TOK)

    first = Dense(c.a["ab_q"], 5, KD, c.h, TOK, scalar=copy_tile(qka), free="scalar")
    mod_norm(c, 0, 1, TOK, first)
    dense_stage(
        c, first,
        Dense(c.a["ab_bq"], 8, KD, c.h, TOK, scalar=copy_tile(qb, BQK), free="scalar", m=BQK),
        Dense(c.a["ab_bkv"], 2, KD, c.h, TOK, scalar=copy_tile(bkv), free="scalar"),
        Dense(c.a["ab_bkr"], 1, KD, c.h, TOK, scalar=copy_tile(bkr, BQK), free="scalar", m=BQK), ahead=True)
    rows_stage(c, KD, [(c.a["ab_v"], 128, c.h, range(4), lambda act, b, bank, m: act.copy(va[:, b], bank))])
    norm_stage(c, bkv, bkv, 2, TOK, lambda k, s: c.v("b_kvn", k), scratch=c.h)

    def key(act, t, g, slot, banks):
        act.copy(kb[64:BQK, bass.ds(t, 1), :], bkr[64:BQK])
        return act.copy(kb[0:64, bass.ds(t, 1), :], split(banks[0], 1, TOK))
    dense_stage(c, Dense(c.a["ab_ukn"], 8, 2, bkv, TOK, scalar=key, free="scalar", m=64))
    rows_stage(c, 2, [(c.a["ab_ukv"], 512, bkv, range(4), lambda act, b, bank, m: act.copy(vb[:, b], bank))])
    heads_stage(
        c, Heads(qka, 5, TOK, c.t("ones64"), HD, c.v("gain_a", 0, 5), (c.t("rotA"), c.t("cosA"), c.t("sinA"))),
        Heads(c.region(2560, 16, TOK)[0:BQK], 16, TOK, c.t("ones")[0:BQK, 0:BQK], BQK, c.v("gain_b", 0, 16)[0:BQK],
              (c.t("rotB")[0:BQK, 0:BQK], c.t("cosB")[0:BQK], c.t("sinB")[0:BQK]), r=BQK))
    o = c.h
    whole = ((0, P),)

    def items(keys, queries_of):
        out = []
        for s in range(2):
            for tb in range(4):
                lo, hi = (0, TOK) if tb < 2 else (SX, TOK)
                out.append(Item(s, tb, [(0, hi - lo, s, lambda i, s=s, lo=lo, hi=hi: keys(i, s)[..., lo:hi])],
                                [(0, hi - lo, None)], softmax_blocks(lo // P, (hi - lo) // P)))
        return out
    attention_stage(
        c, 4, items(lambda i, s: ka[:, 0], None),
        [(s, (64 * s, 64 * s + 64), lambda i, s=s: qa[64 * s:64 * s + 64, bass.ds(i, 1), :]) for s in range(2)],
        lambda b, s: va[:, b, s * 64:s * 64 + 64],
        lambda i: o[:, bass.ds(i, 1), :], TOK)
    attention_stage(
        c, 4, items(lambda i, s: kb[0:BQK, bass.ds(i * 2 + s, 1), :], None),
        [(s, None, lambda i, s=s: qb[0:BQK, bass.ds(i * 2 + s, 1), :]) for s in range(2)],
        [(s, lambda i, s=s: vb[:, :, bass.ds(i * 128 + s * 64, 64)]) for s in range(2)],
        lambda i: o[:, bass.ds(i + 4, 1), :], TOK, r=BQK)
    dense_stage(c, Dense(c.a["ab_out"], KD, KD, o, TOK, vector=residual(c, 0, 5, TOK)))




def decay_stage(core, keys, logf):
    c, nc = core, core.nc
    bounds = split(c.pt[:, 0:2048], 2, 1024)
    lb, rest = c.pt[:, 2048:3072], c.pt[:, 3072:4096]
    with nc.Block(no_gpsimd_drain=True) as block:

        @block.sync
        def _(sp):
            for l in range(2):
                sp.dma_start(bounds[:, l], c.a["lb"][l:l + 1, :].to_broadcast([P, 1024])).then_inc(c.fetched.sem, 16)

        @block.vector
        def _(dv):
            dv.wait_ge(c.fetched.sem, c.fetched.at(32))
            dv.tensor_tensor(bounds[:, 0], bounds[:, 1], bounds[:, 0], ALU.subtract).then_inc(c.ready_a.sem, 1)
            dv.wait_ge(c.ready_b.sem, c.ready_b.at(1))
            steps = Steps(dv, c.dve_step)
            for way in range(2):
                w = slice(way * 512, way * 512 + 512)
                for tb in range(4):
                    n = way * 4 + tb
                    dv.tensor_tensor(keys[:, n], keys[:, n], rest[:, w], ALU.mult)
                    steps.then(dv.tensor_tensor(logf[:, n], logf[:, n], rest[:, w], ALU.mult))
                    steps.then(dv.tensor_tensor(logf[:, n], logf[:, n], lb[:, w], ALU.add))
                    dv.tensor_scalar(logf[:, n], logf[:, n], LN_FLOOR, None, ALU.max).then_inc(c.ready_c.sem, 1)
            c.dve_step.passed(steps.done())

        @block.scalar
        def _(act):
            act.wait_ge(c.ready_a.sem, c.ready_a.at(1))
            act.activation(lb, bounds[:, 0], ACT.Sigmoid)
            act.activation(rest, bounds[:, 0], ACT.Sigmoid, scale=-1.0).then_inc(c.ready_b.sem, 1)
            for n in range(8):
                act.wait_ge(c.ready_c.sem, c.ready_c.at(n + 1))
                act.activation(logf[:, n], logf[:, n], ACT.Ln)
    c.fetched.passed(32)
    c.ready_a.passed(1)
    c.ready_b.passed(1)
    c.ready_c.passed(8)


def recurrence_stage(core, q, keys, logf, v, o):
    c, nc = core, core.nc
    order = [[2, 3, 0, 1], [3, 2, 1, 0]]
    flat = c.w[:].rearrange("p a b -> p (a b)")
    flat_h = c.h[:].rearrange("p a b -> p (a b)")
    ex = split(flat[:, 0:2048], 2, 8, 128)
    qa = [split(x[:, at:at + 2048], 2, 8, 128) for x, at in ((flat, 2048), (flat_h, 0))]
    kb = [split(x[:, at:at + 2048], 2, 8, 128) for x, at in ((flat, 4096), (flat_h, 2048))]
    lst = flat[:, 6144:6656]
    kst = split(flat[:, 6656:6912], 2, 128)
    kd = split(flat[:, 6912:7424], 4, 128)
    ed = split(flat[:, 7424:7936], 4, 128)
    masked = split(c.pt[:, 0:2048], 2, 1024)
    att = split(c.pt[:, 2048:2304], 2, 128)
    qdec = [split(c.pt[:, at:at + 256], 2, 128) for at in (2304, 2560)]
    st = [split(c.pt[:, at:at + 256], 4, 64) for at in (2816, 3072)]
    st0 = c.pt[:, 3328:3392]
    tot = c.pt[:, 3392:3396]
    sums = [c.t(f"sums{way}") for way in range(2)]
    hmask = [c.t(f"hmask{way}") for way in range(2)]
    LEAD, SMALL, SCORES, OUT = 1, 3, (4, 6), 0
    lead_banks = c.ps[:, LEAD:LEAD + 2, :].rearrange("p a n -> p (a n)")
    units = [[(tb, hh) for tb in order[way][2:] for hh in range(2)] for way in range(2)]
    turn = lambda x: x[0] * 2 + x[1]
    early = lambda x: isinstance(x[0], int) and x[0] == 0

    def turns(body, finish):
        body((0, 0), None, (0, 1))

        def rest(i):
            body((i - 1, 1), (i - 1, 0), (i, 0))
            body((i, 0), (i - 1, 1), (i, 1))
        return rest, lambda: (body((3, 1), (3, 0), None), finish((3, 1)))

    with nc.Block(no_gpsimd_drain=True) as block:

        @block.gpsimd
        def _(pool):
            for way in range(2):
                pool.memset(st[way], 0.0).then_inc(c.pool_step.sem, 1)

            def stage(x):
                i, way = x
                u = turn(x)
                pool.wait_ge(c.ready_b.sem, c.ready_b.at(u * 5))
                pool.sem_inc(c.turns.sem, 1)
                pool.tensor_copy(split(lst, 4, 128), logf[:, way * 4:way * 4 + 4, bass.ds(i * 128, 128)]).then_inc(c.ready_a.sem, 1)
                pool.tensor_copy(kst, keys[:, way * 4:way * 4 + 2, bass.ds(i * 128, 128)]).then_inc(c.ready_a.sem, 1)
                if not early(x):
                    pool.wait_ge(c.scores_done.sem, c.scores_done.at(u * 4 - 4))
                    pool.sem_inc(c.turns.sem, 1)
                pool.tensor_copy(qa[way][:, :, 7, :], q[:, bass.ds(i, 1), :]).then_inc(c.ready_a.sem, 1)
            stage((0, 0))
            stage((0, 1))
            with pool.Fori(1, 4) as i:
                stage((i, 0))
                stage((i, 1))

        @block.tensor
        def _(pe):
            def decays(x):
                way, u = x[1], turn(x)
                pe.wait_ge(c.ready_a.sem, c.ready_a.at(u * 3 + 3))
                pe.wait_ge(c.ready_c.sem, c.ready_c.at(u * 5))
                pe.matmul(c.ps[:, LEAD, :], c.t(f"after{way}"), lst, start=True, stop=True).then_inc(c.ready_b.sem, 1)
                pe.wait_ge(c.ready_e.sem, c.ready_e.at(u))
                for tb in range(4):
                    pe.matmul(c.ps[:, SMALL, tb:tb + 1], lst[:, tb * P:(tb + 1) * P], sums[way][:, 1024:1025], start=True, stop=True)
                for tb in range(2):
                    last = pe.transpose(c.ps[:, SMALL, 128 + tb * P:256 + tb * P], kst[:, tb, :], c.t("ident"))
                last.then_inc(c.ready_b.sem, 1)

            def levels(x, n):
                way, u = x[1], turn(x)
                tb = order[way][2 + n]
                pe.wait_ge(c.ready_c.sem, c.ready_c.at(u * 5 + (4 if n else 1)))
                for b in range(2):
                    last = pe.matmul(c.ps[:, LEAD + b, :], lst[:, tb * P:(tb + 1) * P], sums[way][:, b * 512:b * 512 + 512],
                                     start=True, stop=True)
                last.then_inc(c.ready_b.sem, 1)

            def states(x):
                i, way = x
                u = turn(x)
                pe.wait_ge(c.ready_d.sem, c.ready_d.at(u * 3 + 1))
                pe.wait_ge(c.ready_c.sem, c.ready_c.at(u * 5 + 3))
                for n, tb in enumerate(order[way][:3]):
                    last = pe.matmul(c.ps[:, SMALL, n * P:n * P + P], kd[:, tb, :], v[:, tb:tb + 1, bass.ds(i * 128, 128)],
                                     start=True, stop=True)
                last.then_inc(c.ready_b.sem, 1)

            def scores(x, j):
                way, u = x[1], turn(x)
                tb, hh = units[way][j]
                pe.wait_ge(c.ready_d.sem, c.ready_d.at(u * 3 + (2 + j // 2)))
                pe.wait_ge(c.max_ready.sem, c.max_ready.at(u * 4 + (j - 1)))
                r = slice(64 * hh, 64 * hh + 64)
                for lev in range(8):
                    bank = c.ps[:, SCORES[j % 2] + lev // 4, lev % 4 * P:lev % 4 * P + P]
                    last = pe.matmul(bank, kb[way][r, tb, lev, :], qa[way][r, tb, lev, :], start=True, stop=True)
                last.then_inc(c.scores_done.sem, 1)

            def values(x, j):
                i, way = x
                u = turn(x)
                tb, hh = units[way][j]
                if j == 0:
                    pe.wait_ge(c.ready_e.sem, c.ready_e.at(u + 1))
                    pe.wait_ge(c.o_copied.sem, c.o_copied.at(u))
                pe.wait_ge(c.p_ready.sem, c.p_ready.at(u * 4 + (j + 1)))
                dst = c.ps[:, OUT, hh * 128 + tb * 64:hh * 128 + tb * 64 + 64]
                pe.matmul(dst, qdec[way][:, tb, :], st[way][:, j // 2 * 2 + hh, :], start=True, stop=False)
                pe.matmul(dst, att[:, j % 2, :], v[:, tb:tb + 1, bass.ds(i * 128 + hh * 64, 64)],
                          start=False, stop=True).then_inc(c.heads_done.sem, 1)

            def body(x, before, after):
                scores(x, 0)
                if before:
                    values(before, 3)
                scores(x, 1)
                if after:
                    decays(after)
                values(x, 0)
                scores(x, 2)
                if after:
                    levels(after, 0)
                values(x, 1)
                scores(x, 3)
                if after:
                    states(after)
                values(x, 2)
                if after:
                    levels(after, 1)
            decays((0, 0))
            levels((0, 0), 0)
            states((0, 0))
            levels((0, 0), 1)
            rest, end = turns(body, lambda x: values(x, 3))
            with pe.Fori(1, 4) as i:
                rest(i)
            end()

        @block.scalar
        def _(act):
            def lead(x):
                way, u = x[1], turn(x)
                act.wait_ge(c.ready_b.sem, c.ready_b.at(u * 5 + 1))
                act.wait_ge(c.ready_d.sem, c.ready_d.at(u * 3 - 2))
                act.activation(ed, c.ps[:, LEAD, :].rearrange("p (a n) -> p a n", a=4), ACT.Exp).then_inc(c.ready_c.sem, 1)
                act.wait_ge(c.ready_b.sem, c.ready_b.at(u * 5 + 2))
                act.wait_ge(c.ready_e.sem, c.ready_e.at(u))
                act.activation(tot, c.ps[:, SMALL, 0:4], ACT.Exp).then_inc(c.ready_c.sem, 1)
                if not early(x):
                    act.wait_ge(c.scores_done.sem, c.scores_done.at(u * 4 - 4))
                act.copy(kb[way][:, :, 7, :], c.ps[:, SMALL, 128:384].rearrange("p (a n) -> p a n", a=2)).then_inc(c.ready_c.sem, 1)
                for n, tb in enumerate(order[way][2:]):
                    act.wait_ge(c.ready_b.sem, c.ready_b.at(u * 5 + (3, 5)[n]))
                    act.wait_ge(c.ready_d.sem, c.ready_d.at(u * 3))
                    act.activation(ex[:, tb], split(lead_banks, 8, 128), ACT.Exp).then_inc(c.ready_c.sem, 1)
            lead((0, 0))
            lead((0, 1))
            with act.Fori(1, 4) as i:
                lead((i, 0))
                lead((i, 1))

        @block.vector
        def _(dv):
            steps = Steps(dv, c.dve_step)
            dv.wait_ge(c.pool_step.sem, c.pool_step.at(2))

            def decayed_keys(x):
                i, way = x
                u = turn(x)
                dv.wait_ge(c.ready_c.sem, c.ready_c.at(u * 5 + 1))
                dv.wait_ge(c.ready_b.sem, c.ready_b.at(u * 5 - 1))
                dv.tensor_tensor(kd, ed, keys[:, way * 4:way * 4 + 4, bass.ds(i * 128, 128)], ALU.mult).then_inc(c.ready_d.sem, 1)

            def factors(x, n):
                way, u = x[1], turn(x)
                tb = order[way][2 + n]
                dv.wait_ge(c.ready_c.sem, c.ready_c.at(u * 5 + (4 + n)))
                dv.wait_ge(c.ready_a.sem, c.ready_a.at(u * 3 + 3))
                if not early(x):
                    dv.wait_ge(c.heads_done.sem, c.heads_done.at(u * 4 - 4))
                spreadq = qa[way][:, tb, 7:8, :].to_broadcast([P, 7, P])
                spreadk = kb[way][:, tb, 7:8, :].to_broadcast([P, 7, P])
                dv.tensor_tensor(qa[way][:, tb, 0:7, :], ex[:, tb, 0:7, :], spreadq, ALU.mult)
                dv.tensor_tensor(qdec[way][:, tb, :], ex[:, tb, 7, :], qa[way][:, tb, 7, :], ALU.mult)
                dv.tensor_tensor(kb[way][:, tb, 0:7, :], ex[:, tb, 0:7, :], spreadk, ALU.mult).then_inc(c.ready_d.sem, 1)

            def states(x):
                way, u = x[1], turn(x)
                dv.wait_ge(c.ready_b.sem, c.ready_b.at(u * 5 + 4))
                dv.wait_ge(c.ready_c.sem, c.ready_c.at(u * 5 + 2))
                if not early(x):
                    dv.wait_ge(c.heads_done.sem, c.heads_done.at(u * 4 - 4))
                for hh in range(2):
                    r = slice(64 * hh, 64 * hh + 64)
                    new = lambda n: c.ps[r, SMALL, n * P + hh * 64:n * P + hh * 64 + 64]
                    decay = lambda tb: tot[r, tb:tb + 1]
                    first, second = st[way][r, hh, :], st[way][r, 2 + hh, :]
                    steps.then(dv.tensor_copy(st0[r], new(0)))
                    steps.then(dv.scalar_tensor_tensor(first, st0[r], decay(order[way][1]), new(1), ALU.mult, ALU.add))
                    last = dv.scalar_tensor_tensor(second, first, decay(order[way][2]), new(2), ALU.mult, ALU.add)
                last.then_inc(c.ready_e.sem, 1)

            def mask(x, j):
                way, u = x[1], turn(x)
                dv.wait_ge(c.scores_done.sem, c.scores_done.at(u * 4 + (j + 1)))
                banks = c.ps[:, SCORES[j % 2]:SCORES[j % 2] + 2, :].rearrange("p a n -> p (a n)")
                dv.tensor_tensor(masked[:, j % 2, :], banks, hmask[way], ALU.mult).then_inc(c.max_ready.sem, 1)

            def gather(x, j):
                u = turn(x)
                dv.wait_ge(c.max_ready.sem, c.max_ready.at(u * 4 + (j + 1)))
                dv.wait_ge(c.heads_done.sem, c.heads_done.at(u * 4 + (j - 1)))
                dv.tensor_reduce(att[:, j % 2, :], masked[:, j % 2, :].rearrange("p (l t) -> p t l", l=8), AX, ALU.add)\
                  .then_inc(c.p_ready.sem, 1)

            def result(x):
                i, way = x
                dv.wait_ge(c.heads_done.sem, c.heads_done.at(turn(x) * 4 + 4))
                dst = o[:, :, bass.ds(i * 128, 128)].rearrange("p a (h n) -> p h a n", h=2)
                src = c.ps[:, OUT, 0:256].rearrange("p (h a n) -> p h a n", h=2, a=2)
                last = dv.tensor_copy(dst, src) if way == 0 else dv.tensor_tensor(dst, dst, src, ALU.add)
                last.then_inc(c.o_copied.sem, 1)

            def body(x, before, after):
                mask(x, 0)
                if before:
                    result(before)
                gather(x, 0)
                if after:
                    decayed_keys(after)
                mask(x, 1)
                gather(x, 1)
                if after:
                    factors(after, 0)
                mask(x, 2)
                gather(x, 2)
                if after:
                    states(after)
                mask(x, 3)
                gather(x, 3)
                if after:
                    factors(after, 1)
            decayed_keys((0, 0))
            factors((0, 0), 0)
            states((0, 0))
            factors((0, 0), 1)
            rest, end = turns(body, result)
            steps.iterated(1, 8)
            with dv.Fori(1, 4) as i:
                steps.iteration(i - 1, 8)
                rest(i)
            steps.iterated(3, 8)
            end()
            c.dve_step.passed(steps.done())
    c.pool_step.passed(2)
    for n, k in ((c.ready_a, 3), (c.ready_b, 5), (c.ready_c, 5), (c.ready_d, 3), (c.ready_e, 1),
                 (c.max_ready, 4), (c.scores_done, 4), (c.p_ready, 4), (c.heads_done, 4), (c.o_copied, 1)):
        n.passed(8 * k)


def recurrence_out_stage(core, o, gate, dst):
    c, nc = core, core.nc
    sq = c.w[:, 0, 0:1024]
    gn = c.small[:, 64:128]
    ss, = (c.small[:, 128:144],)
    o16, sq16, gate16 = (x.rearrange("p (h d) -> p h d", d=HD) for x in (o.rearrange("p a b -> p (a b)"), sq, gate.rearrange("p a b -> p (a b)")))
    with nc.Block(no_gpsimd_drain=True) as block:

        @block.sync
        def _(sp):
            sp.dma_start(gn, c.a["c_gn"].to_broadcast([P, HD])).then_inc(c.fetched.sem, 16)

        @block.scalar
        def _(act):
            load_ln_exp(nc, act)
            act.activation(sq, o.rearrange("p a b -> p (a b)"), ACT.Square).then_inc(c.square_ready.sem, 1)
            act.wait_ge(c.stat_ready.sem, c.stat_ready.at(1))
            act.activation(ss, ss, ACT.Ln, bias=EPS, scale=1.0 / HD).then_inc(c.act_step.sem, 1)
            act.wait_ge(c.act_step.sem, c.act_step.at(1))
            act.activation(ss, ss, ACT.Exp, scale=-0.5).then_inc(c.rinv_ready.sem, 1)
            for tb in range(2):
                act.wait_ge(c.tile_done.sem, c.tile_done.at(tb + 1))
                act.copy(dst[:, 0:4, tb * P:(tb + 1) * P], c.ps[:, tb, :].rearrange("p (a b) -> p a b", a=4))

        @block.vector
        def _(dv):
            steps = Steps(dv, c.dve_step)
            dv.wait_ge(c.square_ready.sem, c.square_ready.at(1))
            dv.tensor_reduce(ss, sq16, AX, ALU.add).then_inc(c.stat_ready.sem, 1)
            dv.wait_ge(c.rinv_ready.sem, c.rinv_ready.at(1))
            dv.wait_ge(c.fetched.sem, c.fetched.at(16))
            steps.then(dv.tensor_tensor(o16, o16, ss.rearrange("p (h d) -> p h d", d=1).to_broadcast([P, 16, HD]), ALU.mult))
            steps.then(dv.tensor_tensor(o16, o16, gn.rearrange("p (h d) -> p h d", h=1).to_broadcast([P, 16, HD]), ALU.mult))
            dv.tensor_tensor(o16, o16, gate16, ALU.mult).then_inc(c.normed_ready.sem, 1)
            c.dve_step.passed(steps.done())

        @block.tensor
        def _(pe):
            pe.wait_ge(c.normed_ready.sem, c.normed_ready.at(1))
            for tb in range(2):
                for j in range(4):
                    last = pe.transpose(c.ps[:, tb, j * P:(j + 1) * P], o[:, tb, j * P:(j + 1) * P], c.t("ident"))
                last.then_inc(c.tile_done.sem, 1)
    for n in (c.square_ready, c.stat_ready, c.act_step, c.rinv_ready, c.normed_ready):
        n.passed(1)
    c.tile_done.passed(2)
    c.fetched.passed(16)


def bias_stage(core, bias):
    c, nc = core, core.nc
    nh, nr, ncol = 8, 15, 31
    turned = c.w[:].rearrange("p a b -> p (a b)")[:, 0:4096].rearrange("p (a b) -> p a b", a=16)
    window = c.t("window").rearrange("p (a b) -> p a b", a=1).to_broadcast([P, 2, 256])
    with nc.Block(no_gpsimd_drain=True) as block:

        @block.sync
        def _(sp):
            for row in range(4):
                tb, half = divmod(row, 2)
                for h in range(nh):
                    src = bass.AP(tensor=c.a["rpb"].tensor, offset=h * nr * ncol + (7 - row) * ncol + 15 - (GRID - 1),
                                  ap=[[1, GRID], [ncol, 4], [1, GRID]])
                    sp.dma_start(turned[half * 64:half * 64 + 64, tb * 8 + h, :].rearrange("p (a b) -> p a b", a=4), src)\
                      .then_inc(c.fetched.sem, 16)

        @block.tensor
        def _(pe):
            pe.wait_ge(c.fetched.sem, c.fetched.at(16 * 32))
            for n in range(8):
                pe.matmul(c.ps[:, n, :], c.t("turn"), turned[:, 2 * n:2 * n + 2, :], start=True, stop=True)\
                  .then_inc(c.tile_done.sem, 1)

        @block.vector
        def _(dv):
            for n in range(8):
                dv.wait_ge(c.tile_done.sem, c.tile_done.at(n + 1))
                dv.tensor_tensor(bias[:, 2 * n:2 * n + 2, :], c.ps[:, n, :].rearrange("p (a b) -> p a b", a=2), window, ALU.add)
    c.fetched.passed(16 * 32)
    c.tile_done.passed(8)


def mixer_cd(core, stop):
    c = core
    q, keys, logf = c.region(0, 4, SX), c.region(1024, 8, 512), c.region(5120, 8, 512)
    v, gate = c.region(9216, 4, 512), c.region(11264, 2, 512)
    dq, dk, dv_ = c.region(12288, 4, SX), c.region(13312, 4, TOK), c.region(15360, 4, 512)
    o = c.region(17408, 2, 512)

    def silu_tile(act, t, g, slot, banks):
        return act.activation(q[:, bass.ds(t, 1), :], split(banks[0], 1, SX), ACT.Silu)
    first = Dense(c.a["cd_q"], 4, KD, c.h, SX, scalar=silu_tile, free="scalar")
    mod_norm(c, 1, 1, TOK, first)
    dense_stage(
        c, first,
        Dense(c.a["cd_dq"], 4, KD, c.h, SX, scalar=copy_tile(dq), free="scalar"),
        Dense(c.a["cd_dk"], 4, KD, c.h, TOK, scalar=copy_tile(dk), free="scalar"), ahead=True)

    def sigmoids(way):
        def take(act, b, bank, m):
            act.activation(keys[:, way * 4 + b], bank, ACT.Sigmoid, scale=-1.0)
            return act.activation(logf[:, way * 4 + b], bank, ACT.Sigmoid)
        return take
    w = c.a["cd_rows"]
    rows_stage(c, KD, [
        (w[:, 0], 512, c.h, range(4), sigmoids(0)), (w[:, 1], 512, c.h, range(4), sigmoids(1)),
        (w[:, 2], 512, c.h, range(4), lambda act, b, bank, m: act.copy(v[:, b], bank)),
        (w[:, 3], 512, c.h, range(4), lambda act, b, bank, m: act.copy(dv_[:, b], bank)),
        (w[:, 4], 512, c.h, range(2), lambda act, b, bank, m: act.activation(gate[:, b], bank, ACT.Silu))])
    decay_stage(c, keys, logf)
    recurrence_stage(c, q, keys, logf, v, o)
    recurrence_out_stage(c, o, gate, c.h)
    bias = c.region(5120, 16, 256)
    bias_stage(c, bias)
    heads_stage(c, Heads(dq, 4, SX, c.t("ones64"), HD, c.v("gain_d", 0, 4)),
                Heads(dk, 4, TOK, c.t("ones64"), HD, c.v("gain_d", 4, 4)))
    items = [Item(s, tb, [(0, TOK, s, lambda i: dk[:, bass.ds(i, 1), :])], [(0, TOK, None)], softmax_blocks(0, 4),
                  [(256, 256, None), (0, 256, lambda i, s=s, tb=tb: bias[:, bass.ds(i * 2 + (tb * 8 + s), 1), :])])
             for s in range(2) for tb in range(2)]
    attention_stage(
        c, 4, items,
        [(s, (64 * s, 64 * s + 64), lambda i, s=s: dq[64 * s:64 * s + 64, bass.ds(i, 1), :]) for s in range(2)],
        [(s, lambda i, s=s: dv_[:, :, bass.ds(i * 128 + s * 64, 64)]) for s in range(2)],
        lambda i: c.h[:, bass.ds(i + 4, 1), 0:SX], SX)
    dense_stage(c, Dense(c.a["cd_out"], KD, KD, c.h, SX, vector=residual(c, 1, 5, SX)))




def plus(core):
    c = core

    def take(dv, t, g, slot, banks, steps):
        x = c.x[:, bass.ds(t, 1), 0:SX]
        return dv.tensor_tensor(x, x, split(banks[0], 1, SX), ALU.add)
    return take


def mem_stage(core):
    c, nc = core, core.nc
    with nc.Block(no_gpsimd_drain=True) as block:

        @block.sync
        def _(sp):
            sp.dma_start(c.x[:, :, SX:TOK], c.a["mem"]).then_inc(c.fetched.sem, 16)
            sp.wait_ge(c.fetched.sem, c.fetched.at(16))
    c.fetched.passed(16)


def mlp(core, l):
    c = core
    hidden = c.region(0, KF2, SX)

    tmp = split(c.pt[:, 0:1024], 2, 512)

    def relu(act, t, g, slot, banks):
        act.wait_ge(c.psum_free.sem, c.psum_free.at(g - 1))
        return act.activation(tmp[:, slot, 0:SX], banks[0], ACT.Relu).then_inc(c.silu_ready.sem, 1)

    def square(dv, t, g, slot, banks, steps):
        dv.wait_ge(c.silu_ready.sem, c.silu_ready.at(g + 1))
        r = split(tmp[:, slot, 0:SX], 1, SX)
        return dv.tensor_tensor(hidden[:, bass.ds(t, 1), :], r, r, ALU.mult)
    up = Dense(c.a[f"up{l}"], KF2, KD, c.h, SX, vector=square, scalar=relu)
    norm_stage(c, c.x, c.h, KD, SX, lambda k, s: c.v("mlp_norm", l * KD + k), then=up)
    dense_stage(c, up, Dense(c.a[f"down{l}"], KD, KF2, hidden, SX, vector=plus(c), after=True), ahead=True)


def head_queries(t, first=0):
    return [(s, (64 * s, 64 * s + 64), lambda i, s=s: t[64 * s:64 * s + 64, bass.ds(i + first, 1), :]) for s in range(2)]


def memory_attention(core, q, k, v, first):
    c = core
    items = [Item(s, tb, [(0, SC, s, lambda i: k[:, bass.ds(i, 1), :])], [(0, SC, None)], softmax_blocks(0, 2))
             for s in range(2) for tb in range(2)]
    attention_stage(c, 2, items, head_queries(q), [(s, lambda i, s=s: v[:, :, bass.ds(i * 128 + s * 64, 64)]) for s in range(2)],
                    lambda i: c.h[:, bass.ds(i + first, 1), 0:SX], SX)


def compress_stage(core, raw, blocks):
    c, nc = core, core.nc
    with nc.Block(no_gpsimd_drain=True) as block:

        @block.vector
        def _(dv):
            for i in range(2):
                for g in range(3):
                    for par in range(2):
                        r = slice(64 * par, 64 * par + 64)
                        src = raw[r, i * 3 + g, :].rearrange("p (n m r) -> p r m n", r=2, m=8)
                        for half in range(2):
                            pos = c.v("cmp_pos", i * 16 + half * 8, 8)[r].rearrange("p (m n) -> p m n", n=1)
                            dv.tensor_tensor(blocks[r, i * 16 + half * 8:i * 16 + half * 8 + 8, g * NCMP:(g + 1) * NCMP],
                                             src[:, par, :, half:half + NCMP], pos.to_broadcast([64, 8, NCMP]), ALU.add)


def compressed_stage(core, hidden, kc, vc, b2):
    c, nc = core, core.nc
    w = c.w[:, 0, 0:384]
    with nc.Block(no_gpsimd_drain=True) as block:

        @block.sync
        def _(sp):
            sp.dma_start(w, c.a["s_w2"]).then_inc(c.fetched.sem, 16)
            sp.dma_start(b2[0:NCMP], c.a["s_b2v"].to_broadcast([NCMP, HD])).then_inc(c.fetched.sem, 16)

        @block.tensor
        def _(pe):
            pe.wait_ge(c.fetched.sem, c.fetched.at(32))
            for k in range(2):
                pe.matmul(c.ps[:, 0, 0:45], w[:, k * P:(k + 1) * P], hidden[:, k, :], start=(k == 0), stop=(k == 1))
            for g in range(3):
                for k in range(2):
                    last = pe.matmul(c.ps[0:NCMP, 1, g * HD:(g + 1) * HD], hidden[:, 2 + k, g * NCMP:(g + 1) * NCMP],
                                     w[:, 256 + k * HD:256 + (k + 1) * HD], start=(k == 0), stop=(k == 1))
            last.then_inc(c.tile_done.sem, 1)

        @block.vector
        def _(dv):
            dv.wait_ge(c.tile_done.sem, c.tile_done.at(1))
            dv.tensor_scalar(kc[:, 0, :], c.ps[:, 0, 0:45], c.v("cmp_b2"), None, ALU.add)
            for j, g in enumerate((0, 1, 2, 2)):
                dv.tensor_tensor(vc[0:NCMP, j, :], c.ps[0:NCMP, 1, g * HD:(g + 1) * HD], b2[0:NCMP], ALU.add)
    c.tile_done.passed(1)
    c.fetched.passed(32)


def pair_keys_stage(core, kc, kcp, gates):
    c, nc = core, core.nc
    with nc.Block(no_gpsimd_drain=True) as block:

        @block.vector
        def _(dv):
            dv.tensor_copy(kcp[0:64, 0, :], kc[0:64, 0, 0:NCMP])
            dv.tensor_copy(kcp[64:P, 0, :], kc[64:P, 0, NCMP:2 * NCMP])
            dv.tensor_copy(kcp[:, 1, :], kc[:, 0, 2 * NCMP:3 * NCMP])
            for tb in range(2):
                g = gates[:, tb, :].rearrange("p (h b) -> p h b", b=3)[:, :, 2]
                dv.tensor_scalar(g, g, c.t("cmpany")[:, tb:tb + 1], None, ALU.mult)


def mixer_nsa(core):
    c = core
    qk, mk, raw = c.region(0, 12, SX), c.region(3072, 2, SC), c.region(3584, 6, SX)
    v, gates, mv = c.region(5120, 2, 512), c.region(6144, 2, 36), c.region(6216, 2, 256)
    blocks, hidden = c.region(6728, 32, 45), c.region(8168, 4, 45)
    kc, kcp, vc = c.region(8348, 1, 45), c.region(8393, 2, NCMP), c.region(8423, 4, HD)
    b2 = c.region(8679, HD)
    mem = c.h[:, :, SX:TOK]
    q, ksel, kwin, mq = qk[:, 0:6], qk[:, 6:8], qk[:, 8:10], qk[:, 10:12]
    job = Dense(c.a["s_q"], 12, KD, c.h, SX, scalar=copy_tile(qk), free="scalar")
    norm_stage(c, c.x, c.h, KD, TOK, lambda k, s: c.v(("attn_norm", "mem_norm")[s], k), then=job)
    dense_stage(
        c, job,
        Dense(c.a["s_cmp"], 6, KD, c.h, SX, scalar=copy_tile(raw), free="scalar"),
        Dense(c.a["memk0"], 2, KD, mem, SC, scalar=copy_tile(mk), free="scalar"), ahead=True)
    rows_stage(c, KD, [
        (c.a["s_v"], 512, c.h, range(2), lambda act, b, bank, m: act.copy(v[:, b], bank)),
        (c.a["s_g"], 36, c.h, range(2), lambda act, b, bank, m: act.activation(gates[:, b], bank, ACT.Sigmoid)),
        (c.a["memv0"], 256, mem, range(2), lambda act, b, bank, m: act.copy(mv[:, b], bank))])
    compress_stage(c, raw, blocks)

    def gelu(i):
        def take(act, t, g, slot, banks):
            return act.activation(hidden[:, bass.ds(t + i * 2, 1), :], split(banks[0], 1, 45), ACT.Gelu_apprx_tanh,
                                  bias=c.v("cmp_b1", i * 2, 2)[:, bass.ds(t, 1)])
        return take
    dense_stage(c, *[Dense(c.a["s_w1"][:, i], 2, 16, blocks[:, i * 16:(i + 1) * 16], 45, scalar=gelu(i), free="scalar")
                     for i in range(2)])
    compressed_stage(c, hidden, kc, vc, b2)
    rot = (c.t("rotS"), c.t("cosS"), c.t("sinS"))
    heads_stage(c, Heads(qk, 10, SX, c.t("ones64"), HD, c.v("gain_s", 0, 10), rot),
                Heads(kc, 1, 45, c.t("ones64"), HD, c.v("gain_c"), (c.t("rotS"), c.t("cosC"), c.t("sinC"))))
    heads_stage(c, Heads(c.region(2560, 4, SX), 4, SX, c.t("ones64"), HD, c.v("gain_m0", 0, 4)))
    pair_keys_stage(c, kc, kcp, gates)
    for kt, first, n in ((0, 0, 4), (1, 4, 2)):
        items = []
        for s in range(2):
            for tb in range(2):
                w = (tb + 1) * P
                mask = split(c.t(f"nsa{tb}")[:, 0:512], 2, 256)[:, :, 0:w]
                few = split(c.t(f"nsa{tb}")[:, 512:], 1, NCMP)
                parts = [(0, w), (w, w), (512, NCMP)]
                keys = [lambda i, w=w: ksel[:, kt, 0:w], lambda i, w=w: kwin[:, kt, 0:w], lambda i: kcp[:, kt, :]]
                base = (first * 2 + s) * 3
                gate = lambda i, tb=tb, base=base: gates[:, tb, bass.ds(i * 6 + base, 3)]
                items.append(Item(
                    s, tb, [(a, n_, s, key) for (a, n_), key in zip(parts, keys)], [(a, a + n_, gate) for a, n_ in parts],
                    [(b * P, P, b) for b in range(tb + 1)] + [(w + b * P, P, 2 + b) for b in range(tb + 1)] + [(512, NCMP, 4)],
                    [(0, 2 * w, lambda i, mask=mask: mask), (512, NCMP, lambda i, few=few: few)]))

        def values(b, s, kt=kt):
            return vc[0:NCMP, kt * 2 + s, :] if b == 4 else v[:, b % 2, (b // 2) * 256 + kt * 128 + s * 64:][:, 0:64]
        attention_stage(c, n, items, head_queries(q, first), values,
                        lambda i, first=first: c.h[:, bass.ds(i + first, 1), 0:SX], SX)
    memory_attention(c, mq, mk, mv, 6)
    dense_stage(c, Dense(c.a["s_out"], KD, KD, c.h, SX, vector=plus(c)))


def mixer_dilated(core):
    c = core
    hk = c.region(0, KD, SX)
    norm_stage(c, c.x, hk, KD, SX, lambda k, s: c.v("kv_norm", k))
    k, q, mk = c.region(2048, 4, SX), c.region(3072, 14, SX), c.region(6656, 2, SC)
    v, mv = c.region(7168, 2, 512), c.region(8192, 2, 256)
    mem = c.h[:, :, SX:TOK]
    mq = q[:, 12:14]
    job = Dense(c.a["d_k"], 4, KD, hk, SX, scalar=copy_tile(k), free="scalar")
    norm_stage(c, c.x, c.h, KD, TOK, lambda k, s: c.v(("attn_norm", "mem_norm")[s], KD + k), then=job)
    dense_stage(
        c, job,
        Dense(c.a["d_q"], 14, KD, c.h, SX, scalar=copy_tile(q), free="scalar"),
        Dense(c.a["memk1"], 2, KD, mem, SC, scalar=copy_tile(mk), free="scalar"), ahead=True)
    rows_stage(c, KD, [
        (c.a["d_v"], 512, hk, range(2), lambda act, b, bank, m: act.copy(v[:, b], bank)),
        (c.a["memv1"], 256, mem, range(2), lambda act, b, bank, m: act.copy(mv[:, b], bank))])
    rot = (c.t("rotS"), c.t("cosS"), c.t("sinS"))
    heads_stage(c, Heads(c.region(2048, 16, SX), 16, SX, c.t("ones64"), HD, c.v("gain_g", 0, 16), rot))
    heads_stage(c, Heads(c.region(6144, 4, SX), 4, SX, c.t("ones64"), HD, c.v("gain_m1", 0, 4)))
    items = []
    for s in range(2):
        for tb in range(2):
            w = (tb + 1) * P
            mask = split(c.t(f"dil{tb}"), 3, 256)[:, :, 0:w]
            items.append(Item(
                s, tb, [(g * w, w, g * 2 + s, lambda i, w=w: k[:, bass.ds(i, 1), 0:w]) for g in range(3)], [(0, 3 * w, None)],
                softmax_blocks(0, tb + 1),
                [(0, 3 * w, lambda i, mask=mask: mask)],
                fold=w))
    queries = [x for g in range(3) for x in head_queries(q, g * 4)]
    attention_stage(c, 4, items, queries, [(s, lambda i, s=s: v[:, :, bass.ds(i * 128 + s * 64, 64)]) for s in range(2)],
                    lambda i: c.h[:, bass.ds(i, 1), 0:SX], SX)
    memory_attention(c, mq, mk, mv, 4)
    dense_stage(c, Dense(c.a["d_out"], KD, 6, c.h, SX, vector=plus(c)))





def program(nc, args, out, v_at, c_at, stop=None):
    with ExitStack() as ctx:
        c = Core(nc, ctx, args, v_at, c_at)
        build(c, stop)
        with nc.Block(no_gpsimd_drain=True) as block:

            @block.sync
            def _(sp):
                sp.dma_start(out, c.x[:, :, 0:out.shape[2]]).then_inc(c.stored.sem, 16)
                sp.wait_ge(c.stored.sem, c.stored.at(16))


def build(c, stop=None):
    def at(name):
        return stop == name
    load_stage(c)
    ada_stage(c)
    gain_stage(c)
    ffn(c, 0, 0, TOK)
    if at("ffn00"):
        return
    mixer_ab(c, stop)
    if at("mix0"):
        return
    ffn(c, 0, 1, TOK)
    if at("ffn01x"):
        return
    ffn(c, 1, 0, TOK)
    if at("ffn10"):
        return
    mixer_cd(c, stop)
    if at("mix1"):
        return
    ffn(c, 1, 1, SX)
    if at("first"):
        return
    mem_stage(c)
    mixer_nsa(c)
    if at("attn0"):
        return
    mlp(c, 0)
    mixer_dilated(c)
    if at("attn1"):
        return
    mlp(c, 1)


def kernel(**inputs):
    import concourse.bacc as bacc
    from concourse.bass_utils import run_bass_kernel_spmd

    arrays, v_at, c_at = layout(inputs)
    nc = bacc.Bacc("TRN2", target_bir_lowering=False, num_devices=1)
    args = {n: nc.dram_tensor(f"in_{n}", v.shape, mybir.dt.from_np(v.dtype), kind="ExternalInput").ap()
            for n, v in arrays.items()}
    out = nc.dram_tensor("out_x", (P, KD, SX), F32, kind="ExternalOutput").ap()
    program(nc, args, out, v_at, c_at)
    run = run_bass_kernel_spmd(nc, [{f"in_{n}": np.ascontiguousarray(v) for n, v in arrays.items()}], core_ids=[0])
    y = run.results[0]["out_x"]
    return np.ascontiguousarray(y.transpose(2, 1, 0)).reshape(1, SX, D)
```
